# Optimizing a Trainium2 kernel written in Bass

```python
import jax, jax.numpy as jnp
from jax import lax
import numpy as np

D_MODEL = 1024
BATCH = 1
SEQ = 512
DEPTH = 1

ATT_HEADS = 8
ATT_HEAD_DIM = 64
ATT_WIDTH = ATT_HEADS * ATT_HEAD_DIM
ROPE_FRACTION_DIV = 4
ATT_ROPE_DIM = ATT_HEAD_DIM // ROPE_FRACTION_DIV
ROPE_THETA = 500000.0
IDX_HEADS = 4
IDX_DIM = 64
IDX_ROPE_DIM = IDX_DIM // ROPE_FRACTION_DIV
TOPK_MAX = 256
Q_BLOCK = 128

RET_HEADS = 4
RET_QK_DIM = 64
RET_V_DIM = 128
RET_QK_WIDTH = RET_HEADS * RET_QK_DIM
RET_V_WIDTH = RET_HEADS * RET_V_DIM
RET_CHUNK = 128
RET_THETA = 10000.0

MIX_WIDTH = ATT_WIDTH + RET_V_WIDTH
SPLITS = (ATT_WIDTH, ATT_WIDTH, ATT_WIDTH, ATT_WIDTH,
          IDX_HEADS * IDX_DIM, IDX_DIM, IDX_HEADS,
          RET_QK_WIDTH, RET_QK_WIDTH, RET_V_WIDTH, RET_V_WIDTH)
IN_WIDTH = 4 * ATT_WIDTH + IDX_HEADS * IDX_DIM + IDX_DIM + IDX_HEADS + 2 * RET_QK_WIDTH + 2 * RET_V_WIDTH
EPS = 1e-6

kernel_name = "hymba_dsa_retention_gated_layer"

def rms_norm(x, g):
    xf = x.astype(jnp.float32)
    y = xf * lax.rsqrt(jnp.mean(xf * xf, axis=-1, keepdims=True) + EPS)
    return (y * g.astype(jnp.float32)).astype(x.dtype)

def rotary(x, pos, rot_dim, theta):
    half = rot_dim // 2
    inv = 1.0 / (theta ** (jnp.arange(half, dtype=jnp.float32) / half))
    ang = pos.astype(jnp.float32)[:, None] * inv[None, :]
    cos = jnp.cos(ang)[:, None, :]
    sin = jnp.sin(ang)[:, None, :]
    xr = x[..., :rot_dim].astype(jnp.float32)
    x1, x2 = xr[..., :half], xr[..., half:]
    rot = jnp.concatenate([x1 * cos - x2 * sin, x2 * cos + x1 * sin], axis=-1).astype(x.dtype)
    return jnp.concatenate([rot, x[..., rot_dim:]], axis=-1)

def dsa_attention(q, k, v, q_idx, k_idx, w_idx, topk):
    B, S, H, hd = q.shape
    n_blocks = S // Q_BLOCK
    s_pos = jnp.arange(S)
    k_idx_f = k_idx.astype(jnp.float32)

    def block(i):
        start = i * Q_BLOCK
        qb = lax.dynamic_slice_in_dim(q, start, Q_BLOCK, axis=1)
        qib = lax.dynamic_slice_in_dim(q_idx, start, Q_BLOCK, axis=1)
        wb = lax.dynamic_slice_in_dim(w_idx, start, Q_BLOCK, axis=1)
        t = start + jnp.arange(Q_BLOCK)
        logits = jnp.einsum('bqhd,bsd->bqhs', qib.astype(jnp.float32), k_idx_f) * (IDX_DIM ** -0.5)
        score = jnp.einsum('bqh,bqhs->bqs', wb.astype(jnp.float32) * (IDX_HEADS ** -0.5),
                           jax.nn.relu(logits))
        causal = s_pos[None, :] <= t[:, None]
        score = jnp.where(causal[None], score, -jnp.inf)
        _, sel = lax.top_k(score, topk)
        valid = sel <= t[None, :, None]
        kg = jax.vmap(lambda kb, ib: kb[ib])(k, sel)
        vg = jax.vmap(lambda vb, ib: vb[ib])(v, sel)
        att = jnp.einsum('bqhd,bqkhd->bhqk', qb.astype(jnp.float32),
                         kg.astype(jnp.float32)) * (hd ** -0.5)
        att = jnp.where(valid[:, None], att, -jnp.inf)
        p = jax.nn.softmax(att, axis=-1)
        out = jnp.einsum('bhqk,bqkhd->bqhd', p, vg.astype(jnp.float32))
        return out.astype(q.dtype)

    outs = lax.map(block, jnp.arange(n_blocks))
    return outs.transpose(1, 0, 2, 3, 4).reshape(B, S, H, hd)

def retention(q, k, v):
    B, S, H, dk = q.shape
    dv = v.shape[-1]
    C = RET_CHUNK
    N = S // C
    gamma = 1.0 - 2.0 ** (-5.0 - jnp.arange(H, dtype=jnp.float32))
    log_g = jnp.log(gamma)
    qf = q.astype(jnp.float32).reshape(B, N, C, H, dk)
    kf = (k.astype(jnp.float32) * (dk ** -0.5)).reshape(B, N, C, H, dk)
    vf = v.astype(jnp.float32).reshape(B, N, C, H, dv)
    idx = jnp.arange(C, dtype=jnp.float32)
    diff = idx[:, None] - idx[None, :]
    decay = jnp.where(diff[None] >= 0,
                      jnp.exp(log_g[:, None, None] * jnp.maximum(diff, 0.0)[None]), 0.0)
    scores = jnp.einsum('bnihd,bnjhd->bnhij', qf, kf) * decay[None, None]
    inner = jnp.einsum('bnhij,bnjhe->bnihe', scores, vf)
    zeta = jnp.exp(log_g[:, None] * (C - 1.0 - idx)[None, :])
    kv = jnp.einsum('bnjhd,hj,bnjhe->bnhde', kf, zeta, vf)
    g_chunk = jnp.exp(log_g * C)[None, :, None, None]

    def step(state, kv_n):
        return state * g_chunk + kv_n, state

    _, r_prev = lax.scan(step, jnp.zeros((B, H, dk, dv), jnp.float32), kv.transpose(1, 0, 2, 3, 4))
    r_prev = r_prev.transpose(1, 0, 2, 3, 4)
    xi = jnp.exp(log_g[:, None] * (idx + 1.0)[None, :])
    cross = jnp.einsum('bnihd,hi,bnhde->bnihe', qf, xi, r_prev)
    out = (inner + cross).reshape(B, S, H, dv)
    out = out * lax.rsqrt(jnp.mean(out * out, axis=-1, keepdims=True) + EPS)
    return out.astype(q.dtype)

def setup_inputs(seed: int = 0) -> dict:
    key = jax.random.key(seed)
    kx, kg, kin, kout, kf = jax.random.split(key, 5)
    x = jax.random.normal(kx, (BATCH, SEQ, D_MODEL), jnp.float32)
    norm_gain = 1.0 + 0.02 * jax.random.normal(kg, (DEPTH, D_MODEL), jnp.float32)
    w_in = jax.random.normal(kin, (DEPTH, D_MODEL, IN_WIDTH), jnp.float32) * (D_MODEL ** -0.5)
    w_out = jax.random.normal(kout, (DEPTH, MIX_WIDTH, D_MODEL), jnp.float32) * (MIX_WIDTH ** -0.5)
    final_gain = 1.0 + 0.02 * jax.random.normal(kf, (D_MODEL,), jnp.float32)
    return {"x": x, "norm_gain": norm_gain, "w_in": w_in, "w_out": w_out, "final_gain": final_gain}

def reference(x, norm_gain, w_in, w_out, final_gain):
    B, S, _ = x.shape
    pos = jnp.arange(S)
    topk = min(TOPK_MAX, S // 4)
    split_points = np.cumsum(SPLITS)[:-1].tolist()
    h = x
    for layer in range(DEPTH):
        u = rms_norm(h, norm_gain[layer])
        z = jnp.einsum('bsd,de->bse', u, w_in[layer])
        (q_a, k_a, v_a, g_a, q_i, k_i, w_i, q_r, k_r, v_r, g_r) = jnp.split(z, split_points, axis=-1)
        q_a = rotary(q_a.reshape(B, S, ATT_HEADS, ATT_HEAD_DIM), pos, ATT_ROPE_DIM, ROPE_THETA)
        k_a = rotary(k_a.reshape(B, S, ATT_HEADS, ATT_HEAD_DIM), pos, ATT_ROPE_DIM, ROPE_THETA)
        v_a = v_a.reshape(B, S, ATT_HEADS, ATT_HEAD_DIM)
        q_i = rotary(q_i.reshape(B, S, IDX_HEADS, IDX_DIM), pos, IDX_ROPE_DIM, ROPE_THETA)
        k_i = rotary(k_i.reshape(B, S, 1, IDX_DIM), pos, IDX_ROPE_DIM, ROPE_THETA)[:, :, 0, :]
        y_a = dsa_attention(q_a, k_a, v_a, q_i, k_i, w_i, topk).reshape(B, S, ATT_WIDTH)
        y_a = y_a * jax.nn.silu(g_a)
        q_r = rotary(q_r.reshape(B, S, RET_HEADS, RET_QK_DIM), pos, RET_QK_DIM, RET_THETA)
        k_r = rotary(k_r.reshape(B, S, RET_HEADS, RET_QK_DIM), pos, RET_QK_DIM, RET_THETA)
        v_r = v_r.reshape(B, S, RET_HEADS, RET_V_DIM)
        y_r = retention(q_r, k_r, v_r).reshape(B, S, RET_V_WIDTH)
        y_r = y_r * jax.nn.silu(g_r)
        mix = jnp.concatenate([y_a, y_r], axis=-1)
        h = h + jnp.einsum('bse,ed->bsd', mix, w_out[layer])
    return rms_norm(h, final_gain)


_drawn_inputs = setup_inputs


def setup_inputs(seed=0):
    import zlib

    import numpy as np

    out = dict(_drawn_inputs(seed))
    spreads = {}
    factors = {'norm_gain': 2.987, 'final_gain': 2.874}
    for name, (base, spread) in spreads.items():
        noise = np.random.default_rng([zlib.crc32(name.encode()), seed]).standard_normal(out[name].shape)
        drawn = base * np.exp(spread * noise) if base else spread * noise
        out[name] = __import__('jax').numpy.asarray(drawn.astype(out[name].dtype))
    for name, factor in factors.items():
        out[name] = (out[name] * factor).astype(out[name].dtype)
    return out
```

```python
from contextlib import ExitStack

import numpy as np

import concourse.bass as bass
from concourse import mybir

F32 = mybir.dt.float32
F32R = mybir.dt.float32r
ALU = mybir.AluOpType
ACT = mybir.ActivationFunctionType

P = 128
SEQ, D_MODEL = 512, 1024
MT = SEQ // P
KT = D_MODEL // P
HEADS, HD = 8, 64
ATT_W = HEADS * HD
IDX_HEADS, IDX_DIM = 4, 64
ROPE_HALF = HD // 4 // 2
ROPE_THETA = 500000.0
TOPK = min(256, SEQ // 4)
RH, RQK, RV = 4, 64, 128
RET_THETA = 10000.0
RET_HALF = RQK // 2
EPS = 1e-6
MASKED = -1e30
TAKEN = -3e38
NEVER = -2e38

IDX_W = IDX_HEADS * IDX_DIM + IDX_DIM + IDX_HEADS
BASE = 4 * ATT_W
CHUNKS = [("idx", BASE, IDX_W), ("q", 0, ATT_W), ("k", ATT_W, ATT_W), ("v", 2 * ATT_W, ATT_W),
          ("ret_qk", BASE + IDX_W, 2 * RH * RQK),
          ("ret_v", BASE + IDX_W + 2 * RH * RQK, RH * RV),
          ("ret_gate", BASE + IDX_W + 2 * RH * RQK + RH * RV, RH * RV),
          ("att_gate", 3 * ATT_W, ATT_W)]
NCH = len(CHUNKS)
CW = 512
KH = KT // 2
UNITS = 2 * NCH + 4
RAW, RING = 2, 4
GROUPS = NCH * MT
OUT_GROUPS = 2 * MT
C_V, C_RQK, C_RV, C_RG, C_AG = 3, 4, 5, 6, 7
ATT0 = MT * C_RQK
PAIRS = HEADS // 2
STEPS = MT * PAIRS
RET0 = MT * C_RG
TOPK0 = 6
ROUNDS = TOPK // 8
PER_SLOT = 4

TAB = {}
_at = 0
for _n, _w in (("ident", P), ("att_cos", MT * ROPE_HALF), ("att_sin", MT * 2 * ROPE_HALF),
               ("ret_cos", MT * RET_HALF), ("ret_sin", MT * 2 * RET_HALF), ("decay", RH * P),
               ("xi", 2 * P), ("zeta", RH), ("g_chunk", 2), ("causal", P)):
    TAB[_n] = (_at, _at + _w)
    _at += _w
TAB_W = _at


def tables():
    t = np.zeros((P, TAB_W), np.float32)

    def put(name, a):
        lo, hi = TAB[name]
        t[:, lo:hi] = np.asarray(a, np.float32).reshape(P, hi - lo)

    def rope(half, theta):
        inv = np.float32(1.0) / (np.float32(theta) ** (np.arange(half, dtype=np.float32) / np.float32(half)))
        ang = (np.arange(SEQ, dtype=np.float32)[:, None] * inv[None, :]).astype(np.float32).astype(np.float64)
        c = np.cos(ang).reshape(MT, P, half).transpose(1, 0, 2)
        s = np.sin(ang).reshape(MT, P, half).transpose(1, 0, 2)
        return c, np.stack([-s, s], axis=2)

    put("ident", np.eye(P))
    c, s = rope(ROPE_HALF, ROPE_THETA)
    put("att_cos", c), put("att_sin", s)
    c, s = rope(RET_HALF, RET_THETA)
    put("ret_cos", c), put("ret_sin", s)
    log_g = np.log((1.0 - 2.0 ** (-5.0 - np.arange(RH))).astype(np.float32)).astype(np.float64)
    i = np.arange(P, dtype=np.float64)
    diff = i[None, :] - i[:, None]
    decay = np.where(diff[None] >= 0, np.exp(log_g[:, None, None] * np.maximum(diff, 0)), 0.0)
    put("decay", decay.transpose(1, 0, 2) * RQK ** -0.5)
    xi = np.exp(log_g[:, None] * (i + 1.0)[None, :])
    put("xi", np.repeat(xi.reshape(2, 2, P), RQK, axis=1).transpose(1, 0, 2))
    put("zeta", (np.exp(log_g[:, None] * (P - 1.0 - i)[None, :]) * RQK ** -0.5).T)
    put("g_chunk", np.repeat(np.exp(log_g * P).reshape(2, 2), RQK, axis=1).T)
    put("causal", np.where(i[None, :] <= i[:, None], 0.0, MASKED))
    return t


def unit_source(u, w_in, w_out):
    if u < 2 * NCH:
        _, c0, w = CHUNKS[u // 2]
        src = w_in[0]
    else:
        c0, w, src = CW * ((u - 2 * NCH) // 2), CW, w_out[0]
    k0 = KH * (u % 2)
    return src[k0 * P:(k0 + KH) * P, c0:c0 + w].rearrange("(k p) c -> p k c", p=P), w


def splits_at(slot):
    if slot == GROUPS:
        return [UNITS - 2, UNITS - 1]
    if slot < GROUPS and slot % MT == 0:
        return [2 * (slot // MT + 1)]
    if slot < GROUPS and slot % MT == 2:
        return [2 * (slot // MT + 1) + 1]
    return []


def transposed(g):
    c = g // MT
    if g < 0 or g >= GROUPS or c not in (0, 1, 2, C_RQK):
        return None
    return g if c < 3 else g - MT


def hymba_layer(nc, x, norm_gain, w_in, w_out, final_gain, table, out):
    with ExitStack() as ctx:
        def sb(name, shape, dt=F32):
            return ctx.enter_context(nc.sbuf_tensor(name, shape, dt))

        def sem(name):
            return ctx.enter_context(nc.semaphore(name))

        tab = sb("tab", [P, TAB_W])
        xT_hi = sb("xT_hi", [P, KT, SEQ], F32R)
        xT_lo = sb("xT_lo", [P, KT, SEQ], F32R)
        w_raw = sb("w_raw", [P, RAW, KH * CW])
        w_hi = sb("w_hi", [P, RING, KH * CW], F32R)
        w_lo = sb("w_lo", [P, RING, KH * CW], F32R)
        x_qkT = sb("x_qkT", [P, 2 * PAIRS * SEQ])
        x_in = x_qkT[:, :].rearrange("p (m d) -> p m d", m=MT)
        qT = x_qkT[:, 0:PAIRS * SEQ].rearrange("p (a t) -> p a t", a=PAIRS)
        kT = x_qkT[:, PAIRS * SEQ:].rearrange("p (a t) -> p a t", a=PAIRS)
        retT = sb("retT", [P, 6, SEQ])
        qrT, krT, qxT = retT[:, 0:2, :], retT[:, 2:4, :], retT[:, 4:6, :]
        idxT = retT[:, 0:3, :]
        v_att = sb("v_att", [P, MT, ATT_W])
        v_ret = sb("v_ret", [P, MT, RH * RV])
        kz = sb("kz", [P, MT, RH * RQK])
        zt = sb("zt", [P, 2, CW])
        w_idx = sb("w_idx", [P, MT, IDX_HEADS])
        keys = [None] + [sb(f"keys{b}", [P, (b + 1) * P]) for b in range(1, MT)]
        top8 = sb("top8", [P, 8])
        work = sb("work", [P, 4, SEQ])
        prob = work[:, 0:2, :]
        probT = work[:, 2:4, :]
        mix = sb("mix", [P, MT, 2 * ATT_W])
        th = sb("th", [P, CW])
        tmp = sb("tmp", [P, CW])
        rope_a, rope_b = th, tmp
        junk = sb("junk", [P, CW])
        st_sb = sb("st_sb", [P, RH * P])
        state = zt[:, :, :].rearrange("p n (a e) -> p n a e", a=2)
        small = sb("small", [P, 128])
        gain_rows = st_sb[0:KT, 0:P]
        gain = small[:, 0:8]
        ssq, rstd, half_rstd = small[:, 8:12], small[:, 12:16], small[:, 16:20]
        row_max = small[:, 20:22]
        neg_max = small[:, 22:24]
        den = small[:, 24:40].rearrange("p (b h) -> p b h", b=2)
        rden, acoef = small[:, 40:48], small[:, 48:56]
        ret_ms, ret_r, rcoef = small[:, 56:60], small[:, 60:64], small[:, 64:68]
        out_ms, out_ms1, out_rstd = small[:, 68:76], small[:, 76:80], small[:, 80:84]
        minus_half, ms_eps = small[:, 84:88], small[:, 88:92]
        x_again = w_raw[:, 0, :].rearrange("p (m d) -> p m d", m=2)
        fgain = w_raw[:, 1, 0:D_MODEL]
        h_out = x_qkT[:, :].rearrange("p (m d) -> p m d", m=MT)

        bank = [ctx.enter_context(nc.psum_tensor(f"bank{i}", [P, 512], F32)) for i in range(8)]
        proj_ps, score_ps, trans_ps, att_ps, mid_ps = bank[0:2], bank[2:4], bank[4:6], bank[6], bank[7]

        tab_in, x_loaded, gain_in = sem("tab_in"), [sem(f"x_in{m}") for m in range(MT)], sem("gain_in")
        raw_in = [sem(f"raw_in{i}") for i in range(RAW)]
        again_in, fgain_in, stored = [sem(f"again_in{i}") for i in range(MT)], sem("fgain_in"), sem("stored")
        gain_t, gain_ok, xt_done, xhi_done, xlo_done = (sem(n) for n in ("gain_t", "gain_ok", "xt_done", "xhi_done", "xlo_done"))
        sq_done, minus_half_done, rstd_done, hrstd_done = (sem(n) for n in ("sq_done", "minus_half_done", "rstd_done", "hrstd_done"))
        whi_done, wlo_done, proj_done = sem("whi_done"), sem("wlo_done"), sem("proj_done")
        z_done, w_idx_done = sem("z_done"), sem("w_idx_done")
        rope_step, rope_done, t_done, t_evac, qx_done = (sem(n) for n in ("rope_step", "rope_done", "t_done", "t_evac", "qx_done"))
        idx_mm, relu_done, score_step, round_step, mask_done = (sem(n) for n in ("idx_mm", "relu_done", "score_step", "round_step", "mask_done"))
        qk_done, max_done, negmax_done, exp_done = (sem(n) for n in ("qk_done", "max_done", "negmax_done", "exp_done"))
        pt_done, pt_evac, pv_done, att_step, y_att_psum, att_mixed = (sem(n) for n in ("pt_done", "pt_evac", "pv_done", "att_step", "y_att_psum", "att_mixed"))
        tanh_done, rgate_done, agate_psum = (sem(n) for n in ("tanh_done", "rgate_done", "agate_psum"))
        state_zeroed, st_mm, st_evac, kv_mm, state_step, ret_mm, ret_sq, ret_step, y_ret_psum, ret_mixed = (
            sem(n) for n in ("state_zeroed", "st_mm", "st_evac", "kv_mm", "state_step", "ret_mm", "ret_sq", "ret_step", "y_ret_psum", "ret_mixed"))
        mixT_mm, mixhi_done, mixlo_done = sem("mixT_mm"), sem("mixhi_done"), sem("mixlo_done")
        h_added, h_sq, h_step, h_ready = sem("h_added"), sem("h_sq"), sem("h_step"), sem("h_ready")

        def T(name):
            lo, hi = TAB[name]
            return tab[:, lo:hi]

        ident = T("ident")
        block = ctx.enter_context(nc.Block())

        def cols(b):
            return (b + 1) * P

        @block.sync
        def _(sp):
            sp.dma_start(gain_rows, norm_gain[0].rearrange("(k p) -> k p", p=P)).then_inc(gain_in, 16)
            for m in range(MT):
                sp.dma_start(x_in[:, m, :], x[0, m * P:(m + 1) * P, :]).then_inc(x_loaded[m], 16)
                if m == 0:
                    sp.dma_start(tab[:, :], table).then_inc(tab_in, 16)
            for u in range(UNITS):
                src, w = unit_source(u, w_in, w_out)
                if u >= RAW:
                    sp.wait_ge(wlo_done, u - RAW + 1)
                dst = w_raw[:, u % RAW, :].rearrange("p (k c) -> p k c", k=KH)[:, :, 0:w]
                sp.dma_start(dst, src).then_inc(raw_in[u % RAW], 16)
            sp.wait_ge(wlo_done, UNITS - 1)
            for m in range(2):
                sp.dma_start(x_again[:, m, :], x[0, m * P:(m + 1) * P, :]).then_inc(again_in[m], 16)
            sp.wait_ge(wlo_done, UNITS)
            sp.dma_start(fgain, final_gain.rearrange("(a d) -> a d", a=1).broadcast_to([P, D_MODEL])).then_inc(fgain_in, 16)
            for m in range(MT):
                if m >= 2:
                    sp.wait_ge(h_added, 2 * (m - 1))
                    sp.dma_start(x_again[:, m % 2, :], x[0, m * P:(m + 1) * P, :]).then_inc(again_in[m], 16)
            for m in range(MT):
                for n in range(2):
                    sp.wait_ge(h_ready, 2 * m + n + 1)
                    sp.dma_start(out[0, m * P:(m + 1) * P, n * CW:(n + 1) * CW],
                                 h_out[:, m, n * CW:(n + 1) * CW]).then_inc(stored, 16)
            sp.wait_ge(stored, 16 * 2 * MT)

        @block.tensor
        def _(pe):
            pe.wait_ge(gain_in, 16)
            pe.wait_ge(tab_in, 16)
            pe.transpose(mid_ps[:, 0:KT], gain_rows, ident[0:KT, 0:KT]).then_inc(gain_t, 1)
            for m in range(MT):
                pe.wait_ge(x_loaded[m], 16)
            for k in range(KT):
                if k == KT - 1:
                    pe.wait_ge(gain_ok, 1)
                for m in range(MT):
                    mm = pe.transpose(bank[k][:, m * P:(m + 1) * P], x_in[:, m, k * P:(k + 1) * P], ident)
                mm.then_inc(xt_done, 1)
            pe.wait_ge(xlo_done, KT)

            def proj(g, half):
                if g < GROUPS:
                    c, m = g // MT, g % MT
                    u, w = 2 * c + half, CHUNKS[c][2]
                else:
                    m, n = (g - GROUPS) // 2, (g - GROUPS) % 2
                    u, w = 2 * NCH + 2 * n + half, CW
                if half == 0:
                    if 2 <= g < MT * C_RG + 2:
                        pe.wait_ge(z_done, g - 1)
                    elif MT * C_RG + 2 <= g < MT * C_AG + 2:
                        pe.wait_ge(rgate_done, g - 2 - MT * C_RG + 1)
                    elif MT * C_AG + 2 <= g < GROUPS + 2:
                        pe.wait_ge(agate_psum, g - 2 - MT * C_AG + 1)
                    elif g >= GROUPS + 2:
                        pe.wait_ge(h_added, g - 2 - GROUPS + 1)
                    if g >= GROUPS:
                        pe.wait_ge(mixlo_done, 2 * (m + 1))
                pe.wait_ge(wlo_done, u + 1)
                o = proj_ps[g % 2][:, 0:w]
                hi = w_hi[:, u % RING, :].rearrange("p (k c) -> p k c", k=KH)
                lo = w_lo[:, u % RING, :].rearrange("p (k c) -> p k c", k=KH)
                for kk in range(KH):
                    k = KH * half + kk
                    xh, xl = (t[:, k, m * P:(m + 1) * P] for t in (xT_hi, xT_lo))
                    first, last = k == 0, k == KT - 1
                    pe.matmul(o, xh, hi[:, kk, 0:w], start=first, stop=False)
                    pe.matmul(o, xh, lo[:, kk, 0:w], start=False, stop=False)
                    mm = pe.matmul(o, xl, hi[:, kk, 0:w], start=False, stop=last)
                if half == 1:
                    mm.then_inc(proj_done, 1)

            def transpose_group(g):
                i = transposed(g)
                if i is None:
                    return
                pe.wait_ge(rope_done, i + 1)
                if i >= 1:
                    pe.wait_ge(t_evac, i)
                for j in range(3 if g < MT else 4):
                    mm = pe.transpose(mid_ps[:, j * P:(j + 1) * P], zt[:, g % 2, j * P:(j + 1) * P], ident)
                mm.then_inc(t_done, 1)

            def index_logits(b):
                pe.wait_ge(t_evac, MT)
                for h in range(IDX_HEADS):
                    n, r = IDX_HEADS * (b - 1) + h, slice(64 * (h % 2), 64 * (h % 2) + 64)
                    if n >= 2:
                        pe.wait_ge(relu_done, n - 1)
                    pe.matmul(score_ps[h % 2][:, 0:cols(b)], idxT[r, h // 2, b * P:(b + 1) * P],
                              idxT[r, 2, 0:cols(b)], start=True, stop=True).then_inc(idx_mm, 1)

            def values(s):
                b, p = s // PAIRS, s % PAIRS
                if p == 0 and b >= 1:
                    pe.wait_ge(y_att_psum, b)
                for hh in range(2):
                    h = 2 * p + hh
                    pe.wait_ge(pt_evac, 2 * s + hh + 1)
                    for j in range(b + 1):
                        mm = pe.matmul(att_ps[:, h * HD:(h + 1) * HD], probT[:, hh, j * P:(j + 1) * P],
                                       v_att[:, j, h * HD:(h + 1) * HD], start=(j == 0), stop=(j == b))
                mm.then_inc(pv_done, 1)

            def transpose_probs(s):
                b = s // PAIRS
                for hh in range(2):
                    pe.wait_ge(exp_done, 2 * s + hh + 1)
                    if s >= 1:
                        pe.wait_ge(pt_evac, 2 * s + hh - 1)
                    if s == STEPS - 2:
                        pe.wait_ge(mixlo_done, hh + 1)
                    for j in range(b + 1):
                        mm = pe.transpose(trans_ps[hh][:, j * P:(j + 1) * P], prob[:, hh, j * P:(j + 1) * P], ident)
                    mm.then_inc(pt_done, 1)

            def scores(s):
                b, p = s // PAIRS, s % PAIRS
                pe.wait_ge(t_evac, 3 * MT)
                for hh in range(2):
                    if s == 0:
                        pe.wait_ge(relu_done, IDX_HEADS * (MT - 1))
                    else:
                        pe.wait_ge(max_done, 2 * s + hh - 1)
                    r = slice(64 * hh, 64 * hh + 64)
                    pe.matmul(score_ps[hh][:, 0:cols(b)], qT[r, p, b * P:(b + 1) * P], kT[r, p, 0:cols(b)],
                              start=True, stop=True).then_inc(qk_done, 1)

            def ret_scores(n):
                pe.wait_ge(t_evac, 4 * MT)
                if n >= 1:
                    pe.wait_ge(y_ret_psum, n)
                for hh in range(2):
                    r = slice(64 * hh, 64 * hh + 64)
                    if hh:
                        pe.wait_ge(st_mm, 2 * n + 1)
                    for h in (hh, hh + 2):
                        mm = pe.matmul(mid_ps[:, h * P:(h + 1) * P], krT[r, h // 2, n * P:(n + 1) * P],
                                       qrT[r, h // 2, n * P:(n + 1) * P], start=True, stop=True)
                    mm.then_inc(st_mm, 1)

            def ret_kv(n):
                pe.wait_ge(st_evac, n + 1)
                for h in range(RH):
                    r = 64 * (h % 2)
                    mm = pe.matmul(mid_ps[r:r + 64, (h // 2) * RV:(h // 2 + 1) * RV],
                                   kz[:, n, h * RQK:(h + 1) * RQK], v_ret[:, n, h * RV:(h + 1) * RV],
                                   start=True, stop=True)
                mm.then_inc(kv_mm, 1)

            def ret_out(n):
                pe.wait_ge(st_evac, n + 1)
                pe.wait_ge(state_step, RH * min(n + 1, MT - 1))
                for p in range(2):
                    if n:
                        pe.matmul(mid_ps[:, 2 * p * RV:2 * (p + 1) * RV], qxT[:, p, n * P:(n + 1) * P],
                                  state[:, (n - 1) % 2, p, :], start=True, stop=False)
                    for h in (2 * p, 2 * p + 1):
                        mm = pe.matmul(mid_ps[:, h * RV:(h + 1) * RV], st_sb[:, h * P:(h + 1) * P],
                                       v_ret[:, n, h * RV:(h + 1) * RV], start=(n == 0), stop=(n == 0 or h % 2 == 1))
                mm.then_inc(ret_mm, 1)

            def transpose_mix(m):
                pe.wait_ge(att_mixed, m + 1)
                pe.wait_ge(ret_mixed, m + 1)
                pe.wait_ge(pt_evac, 2 * (STEPS - 2) if m == 0 else 2 * STEPS)
                for half in range(2):
                    if m >= 1:
                        pe.wait_ge(mixlo_done, 2 * (m - 1) + half + 1)
                    for j in range(KH):
                        e = (KH * half + j) * P
                        mm = pe.transpose(trans_ps[half][:, j * P:(j + 1) * P], mix[:, m, e:e + P], ident)
                    mm.then_inc(mixT_mm, 1)

            for g in range(GROUPS + OUT_GROUPS):
                proj(g, 0)
                if g >= RET0 + 1 and (g - RET0) % 2 == 1 and (g - RET0) // 2 < MT - 1:
                    ret_kv((g - RET0) // 2)
                if g >= GROUPS - 1 and (g - GROUPS + 1) % 2 == 0 and (g - GROUPS + 1) // 2 < MT:
                    transpose_mix((g - GROUPS + 1) // 2)
                proj(g, 1)
                transpose_group(g - 1)
                if MT <= g < 2 * MT - 1:
                    index_logits(g - MT + 1)
                if 0 <= g - ATT0 - 2 < STEPS:
                    values(g - ATT0 - 2)
                if 0 <= g - ATT0 - 1 < STEPS:
                    transpose_probs(g - ATT0 - 1)
                if 0 <= g - ATT0 < STEPS:
                    scores(g - ATT0)
                if RET0 <= g < RET0 + 2 * MT:
                    n = (g - RET0) // 2
                    if (g - RET0) % 2 == 0:
                        ret_scores(n)
                    else:
                        if n == 1:
                            pe.wait_ge(qx_done, MT)
                        ret_out(n)

        @block.scalar
        def _(act):
            def split_hi(u):
                w = unit_source(u, w_in, w_out)[1]
                act.wait_ge(raw_in[u % RAW], 16 * (u // RAW + 1))
                if u >= RING:
                    act.wait_ge(proj_done, MT * (u // 2 - 1))
                s, d = (t.rearrange("p (k c) -> p k c", k=KH)[:, :, 0:w] for t in (w_raw[:, u % RAW, :], w_hi[:, u % RING, :]))
                act.activation(d, s, ACT.Copy).then_inc(whi_done, 1)

            for m in range(MT):
                act.wait_ge(x_loaded[m], 16)
                if m:
                    act.wait_ge(sq_done, m)
                act.activation(mix[:, 0, :], x_in[:, m, :], ACT.Square, scale=D_MODEL ** -0.5,
                               accum_out=ssq[:, m:m + 1]).then_inc(sq_done, 1)
            act.wait_ge(gain_ok, 1)
            for k in range(KT):
                act.wait_ge(xt_done, k + 1)
                act.activation(xT_hi[:, k, :], bank[k][:, :], ACT.Copy, scale=gain[:, k:k + 1]).then_inc(xhi_done, 1)
                if k == 1:
                    split_hi(0)
            split_hi(1)
            act.wait_ge(hrstd_done, 1)

            def project_out(g):
                c, m = g // MT, g % MT
                act.wait_ge(proj_done, g + 1)
                src = proj_ps[g % 2]
                scale = rstd[:, m:m + 1]
                i = transposed(g)
                if i is not None:
                    if i >= 2:
                        act.wait_ge(t_done, i - 1)
                    w = 5 * IDX_DIM if c == 0 else CW
                    if c == 0:
                        act.activation(w_idx[:, m, :], src[:, w:w + IDX_HEADS], ACT.Copy, scale=scale).then_inc(w_idx_done, 1)
                    act.activation(zt[:, g % 2, 0:w], src[:, 0:w], ACT.Copy, scale=scale).then_inc(z_done, 1)
                elif c in (C_V, C_RV):
                    dst = (v_att if c == C_V else v_ret)[:, m, :]
                    act.activation(dst, src[:, :], ACT.Copy, scale=scale).then_inc(z_done, 1)
                else:
                    i = g - MT * C_RG
                    if i > MT:
                        act.wait_ge(agate_psum, i - MT)
                    elif i:
                        act.wait_ge(rgate_done, i)
                    else:
                        act.wait_ge(rope_done, 4 * MT)
                    act.activation(th[:, :], src[:, :], ACT.Tanh, scale=half_rstd[:, m:m + 1]).then_inc(tanh_done, 1)

            def transposed_out(g):
                i = transposed(g)
                if i is None:
                    return
                c, m = g // MT, g % MT
                t = slice(m * P, (m + 1) * P)
                act.wait_ge(t_done, i + 1)
                n = 3 if c == 0 else 4
                src = mid_ps[:, 0:n * P].rearrange("p (a t) -> p a t", a=n)
                dst = {0: idxT, 1: qT, 2: kT, C_RQK: retT[:, 0:4, :]}[c][:, :, t]
                act.activation(dst, src, ACT.Copy).then_inc(t_evac, 1)

            def relus(b):
                for h in range(IDX_HEADS):
                    n = IDX_HEADS * (b - 1) + h
                    act.wait_ge(idx_mm, n + 1)
                    if b >= 2:
                        act.wait_ge(score_step, 5 * (b - 2) + h + 1)
                    act.activation(work[:, h, 0:cols(b)], score_ps[h % 2][:, 0:cols(b)], ACT.Relu).then_inc(relu_done, 1)

            def exps(s):
                b, p = s // PAIRS, s % PAIRS
                act.wait_ge(negmax_done, s + 1)
                if p == 0 and b >= 2:
                    act.wait_ge(y_att_psum, b - 1)
                for hh in range(2):
                    pr = prob[:, hh, 0:cols(b)]
                    act.activation(pr, pr, ACT.Exp, bias=neg_max[:, hh:hh + 1], scale=HD ** -0.5,
                                   accum_out=den[:, b % 2, 2 * p + hh:2 * p + hh + 1]).then_inc(exp_done, 1)

            def probT_out(s):
                b = s // PAIRS
                for hh in range(2):
                    act.wait_ge(pt_done, 2 * s + hh + 1)
                    if s >= 1:
                        act.wait_ge(pv_done, s)
                    elif hh == 0:
                        act.wait_ge(score_step, 5 * (MT - 1))
                    act.activation(probT[:, hh, 0:cols(b)], trans_ps[hh][:, 0:cols(b)], ACT.Copy).then_inc(pt_evac, 1)

            def ret_squares(n):
                act.wait_ge(ret_mm, n + 1)
                for h in range(RH):
                    if h == 0 and n:
                        act.wait_ge(ret_step, 3 * n)
                        act.wait_ge(ret_sq, RH * n)
                    act.activation(junk[:, h * RV:(h + 1) * RV], mid_ps[:, h * RV:(h + 1) * RV], ACT.Square, scale=RV ** -0.5,
                                   accum_out=ret_ms[:, h:h + 1]).then_inc(ret_sq, 1)

            def mix_hi(m):
                act.wait_ge(proj_done, GROUPS - MT + m + 1)
                for half in range(2):
                    act.wait_ge(mixT_mm, 2 * m + half + 1)
                    act.activation(xT_hi[:, KH * half:KH * (half + 1), m * P:(m + 1) * P],
                                   trans_ps[half][:, :].rearrange("p (k t) -> p k t", k=KH), ACT.Copy).then_inc(mixhi_done, 1)

            for g in range(GROUPS + OUT_GROUPS):
                for u in splits_at(g):
                    split_hi(u)
                if g >= GROUPS - 1 and (g - GROUPS + 1) % 2 == 0 and (g - GROUPS + 1) // 2 < MT:
                    mix_hi((g - GROUPS + 1) // 2)
                if g < GROUPS:
                    project_out(g)
                transposed_out(g - 1)
                if MT <= g < 2 * MT - 1:
                    relus(g - MT + 1)
                if 0 <= g - ATT0 - 1 < STEPS:
                    probT_out(g - ATT0 - 1)
                if 0 <= g - ATT0 < STEPS:
                    exps(g - ATT0)
                if RET0 <= g < RET0 + 2 * MT and (g - RET0) % 2 == 1:
                    ret_squares((g - RET0) // 2)
                if g >= GROUPS:
                    i = g - GROUPS
                    act.wait_ge(h_added, i + 1)
                    act.wait_ge(h_sq, i) if i else act.wait_ge(ret_sq, RH * MT)
                    act.activation(junk[:, :], h_out[:, i // 2, (i % 2) * CW:(i % 2 + 1) * CW], ACT.Square,
                                   scale=D_MODEL ** -0.5, accum_out=out_ms[:, i:i + 1]).then_inc(h_sq, 1)

        @block.gpsimd
        def _(pool):
            step = 0

            def xi_times_q(m):
                t = slice(m * P, (m + 1) * P)
                pool.wait_ge(t_evac, 3 * MT + m + 1)
                pool.tensor_tensor(qxT[:, :, t], qrT[:, :, t], T("xi").rearrange("p (a t) -> p a t", a=2),
                                   ALU.mult).then_inc(qx_done, 1)

            def chain(ins):
                nonlocal step
                step += 1
                ins.then_inc(rope_step, 1)
                return step

            def rsqrt(out, ms, eps_at, done, count):
                n = ms.shape[1]
                pool.tensor_scalar(eps_at, ms, EPS, None, ALU.add).then_inc(done, 1)
                pool.wait_ge(done, count + 1)
                pool.tensor_tensor(out, eps_at, minus_half[:, 0:n], ALU.pow).then_inc(done, 1)
                pool.wait_ge(done, count + 2)

            pool.memset(minus_half, -0.5).then_inc(minus_half_done, 1)
            pool.wait_ge(minus_half_done, 1)
            pool.wait_ge(sq_done, MT)
            rsqrt(rstd, ssq, ms_eps, rstd_done, 0)
            pool.tensor_scalar(half_rstd, rstd, 0.5, None, ALU.mult).then_inc(hrstd_done, 1)

            for g in range(GROUPS):
                i = transposed(g)
                if i is None:
                    continue
                c, m = g // MT, g % MT
                ret = c == C_RQK
                heads = 5 if c == 0 else 8
                half = RET_HALF if ret else ROPE_HALF
                z4 = zt[:, g % 2, 0:heads * HD].rearrange("p (h d) -> p h d", h=heads)
                z = z4[:, :, 0:2 * half].rearrange("p h (s e) -> p h s e", s=2)
                ta = rope_a[:, 0:heads * 2 * half].rearrange("p (h s e) -> p h s e", h=heads, s=2)
                tb = rope_b[:, 0:heads * 2 * half].rearrange("p (h s e) -> p h s e", h=heads, s=2)
                cos = T("ret_cos" if ret else "att_cos")[:, m * half:(m + 1) * half]
                sin = T("ret_sin" if ret else "att_sin")[:, 2 * m * half:2 * (m + 1) * half]
                cos = cos.rearrange("p (h e) -> p h e", h=1).broadcast_to([P, heads, half])
                sin = sin.rearrange("p (h s e) -> p h s e", h=1, s=2)
                pool.wait_ge(tab_in, 16)
                zg = g + 1
                pool.wait_ge(z_done, zg)
                pool.wait_ge(rope_done, i) if i else None
                for s in range(2):
                    chain(pool.tensor_tensor(ta[:, :, s, :], z[:, :, s, :], cos, ALU.mult))
                    last = chain(pool.tensor_tensor(tb[:, :, s, :], z[:, :, 1 - s, :],
                                                    sin[:, :, s, :].broadcast_to([P, heads, half]), ALU.mult))
                pool.wait_ge(rope_step, last)
                add = pool.tensor_tensor(z, ta, tb, ALU.add)
                if c in (1, 2):
                    add.then_inc(rope_done, 1)
                    continue
                last = chain(add)
                pool.wait_ge(rope_step, last)
                if c == 0:
                    pool.tensor_copy(zt[:, g % 2, 5 * HD:6 * HD], zt[:, g % 2, 4 * HD:5 * HD]).then_inc(rope_done, 1)
                else:
                    pool.tensor_tensor(kz[:, m, :].rearrange("p (h d) -> p h d", h=RH), z4[:, RH:2 * RH, :],
                                       T("zeta").rearrange("p (h d) -> p h d", d=1).broadcast_to([P, RH, RQK]),
                                       ALU.mult).then_inc(rope_done, 1)
                    if m:
                        xi_times_q(m - 1)
            xi_times_q(MT - 1)
            pool.wait_ge(t_done, 4 * MT)
            pool.memset(zt[:, :, :], 0.0).then_inc(state_zeroed, 1)

            for n in range(MT):
                pool.wait_ge(ret_sq, RH * (n + 1))
                rsqrt(ret_r, ret_ms, ms_eps, ret_step, 3 * n)
                if n:
                    pool.wait_ge(y_ret_psum, n)
                pool.tensor_scalar(rcoef, ret_r, half_rstd[:, n:n + 1], None, ALU.mult).then_inc(ret_step, 1)
                pool.wait_ge(ret_step, 3 * n + 3)
            for m in range(MT):
                pool.wait_ge(h_sq, 2 * m + 2)
                pool.tensor_tensor(out_ms1[:, m:m + 1], out_ms[:, 2 * m:2 * m + 1], out_ms[:, 2 * m + 1:2 * m + 2],
                                   ALU.add).then_inc(h_step, 1)
                pool.wait_ge(h_step, 3 * m + 1)
                rsqrt(out_rstd[:, m:m + 1], out_ms1[:, m:m + 1], ms_eps[:, 0:1], h_step, 3 * m + 1)

        @block.vector
        def _(dve):
            def split_lo(u):
                w = unit_source(u, w_in, w_out)[1]
                dve.wait_ge(whi_done, u + 1)
                s, h, d = (t.rearrange("p (k c) -> p k c", k=KH)[:, :, 0:w]
                           for t in (w_raw[:, u % RAW, :], w_hi[:, u % RING, :].bitcast(F32), w_lo[:, u % RING, :]))
                dve.tensor_tensor(d, s, h, ALU.subtract).then_inc(wlo_done, 1)

            dve.wait_ge(gain_t, 1)
            dve.tensor_copy(gain, mid_ps[:, 0:KT]).then_inc(gain_ok, 1)
            dve.wait_ge(gain_ok, 1)
            for k in range(KT):
                dve.wait_ge(xhi_done, k + 1)
                dve.scalar_tensor_tensor(out=xT_lo[:, k, :], in0=bank[k][:, :], scalar=gain[:, k:k + 1],
                                         in1=xT_hi[:, k, :].bitcast(F32), op0=ALU.mult, op1=ALU.subtract).then_inc(xlo_done, 1)
                if k == 2:
                    split_lo(0)
            split_lo(1)

            def index_scores(b):
                dve.wait_ge(w_idx_done, b + 1)
                for h in range(IDX_HEADS):
                    dve.wait_ge(relu_done, IDX_HEADS * (b - 1) + h + 1)
                    src, w = work[:, h, 0:cols(b)], w_idx[:, b, h:h + 1]
                    if h == 0:
                        ins = dve.tensor_scalar(keys[b][:, :], src, w, None, ALU.mult)
                    else:
                        dve.wait_ge(score_step, 5 * (b - 1) + h)
                        ins = dve.scalar_tensor_tensor(out=keys[b][:, :], in0=src, scalar=w, in1=keys[b][:, :],
                                                       op0=ALU.mult, op1=ALU.add)
                    ins.then_inc(score_step, 1)
                dve.wait_ge(score_step, 5 * (b - 1) + 4)
                diag = keys[b][:, b * P:(b + 1) * P]
                dve.tensor_tensor(diag, diag, T("causal"), ALU.add).then_inc(score_step, 1)

            def topk_round(r):
                b = 1 + r // ROUNDS
                dve.wait_ge(round_step, 2 * r) if r else None
                dve.wait_ge(score_step, 5 * b)
                dve.max(top8[:, :], keys[b][:, :]).then_inc(round_step, 1)
                dve.wait_ge(round_step, 2 * r + 1)
                dve.match_replace(keys[b][:, :], top8[:, :], keys[b][:, :], TAKEN).then_inc(round_step, 1)
                if r % ROUNDS == ROUNDS - 1:
                    dve.wait_ge(round_step, 2 * r + 2)
                    dve.tensor_scalar(keys[b][:, :], keys[b][:, :], NEVER, MASKED, ALU.is_gt, ALU.mult).then_inc(mask_done, 1)

            def masked_max(s):
                b = s // PAIRS
                dve.wait_ge(mask_done, b) if b else None
                if s:
                    dve.wait_ge(negmax_done, s)
                    dve.wait_ge(exp_done, 2 * s)
                for hh in range(2):
                    dve.wait_ge(qk_done, 2 * s + hh + 1)
                    if s:
                        dve.wait_ge(pt_done, 2 * s + hh - 1)
                    if b == 0:
                        mask, o = T("causal"), prob[:, hh, 0:P]
                    else:
                        mask, o = keys[b][:, :], prob[:, hh, 0:cols(b)]
                    dve.tensor_tensor_reduce(out=o, in0=score_ps[hh][:, 0:cols(b)], in1=mask, scale=1.0, scalar=TAKEN,
                                             op0=ALU.add, op1=ALU.max, accum_out=row_max[:, hh:hh + 1]).then_inc(max_done, 1)
                dve.wait_ge(max_done, 2 * s + 2)
                dve.tensor_scalar(neg_max, row_max, -(HD ** -0.5), None, ALU.mult).then_inc(negmax_done, 1)

            tmp_read = [None]

            def gate(g):
                i = g - MT * C_RG
                m, ret = i % MT, i < MT
                dve.wait_ge(tanh_done, i + 1)
                w = slice(ATT_W, 2 * ATT_W) if ret else slice(0, ATT_W)
                straight = ret or m == MT - 1
                if not straight and tmp_read[0]:
                    dve.wait_ge(*tmp_read[0])
                dst = mix[:, m, w] if straight else tmp[:, :]
                dve.scalar_tensor_tensor(out=dst, in0=th[:, :], scalar=1.0, in1=proj_ps[g % 2][:, :], op0=ALU.add,
                                         op1=ALU.mult).then_inc(rgate_done if ret else agate_psum, 1)
                if not straight:
                    dve.wait_ge(agate_psum, m + 1)
                    dve.wait_ge(y_att_psum, m + 1)
                    dve.tensor_tensor(mix[:, m, w], mix[:, m, w], tmp[:, :], ALU.mult).then_inc(att_mixed, 1)
                    tmp_read[0] = (att_mixed, m + 1)

            def attention_out(b):
                dve.wait_ge(pv_done, PAIRS * (b + 1))
                dve.wait_ge(exp_done, 2 * PAIRS * (b + 1))
                if b:
                    dve.wait_ge(y_att_psum, b)
                dve.reciprocal(rden, den[:, b % 2, :]).then_inc(att_step, 1)
                dve.wait_ge(att_step, 2 * b + 1)
                dve.tensor_scalar(acoef, rden, half_rstd[:, b:b + 1], None, ALU.mult).then_inc(att_step, 1)
                dve.wait_ge(att_step, 2 * b + 2)
                co = acoef.rearrange("p (h d) -> p h d", d=1).broadcast_to([P, HEADS, HD])
                src = att_ps[:, :].rearrange("p (h d) -> p h d", h=HEADS)
                half = mix[:, b, 0:ATT_W]
                if b < MT - 1:
                    dve.tensor_tensor(half.rearrange("p (h d) -> p h d", h=HEADS), src, co, ALU.mult).then_inc(y_att_psum, 1)
                else:
                    dve.wait_ge(*tmp_read[0])
                    dve.tensor_tensor(tmp[:, :].rearrange("p (h d) -> p h d", h=HEADS), src, co, ALU.mult).then_inc(y_att_psum, 1)
                    dve.wait_ge(y_att_psum, b + 1)
                    dve.wait_ge(agate_psum, MT)
                    dve.tensor_tensor(half, half, tmp[:, :], ALU.mult).then_inc(att_mixed, 1)
                    tmp_read[0] = (att_mixed, MT)

            def decayed(n):
                dve.wait_ge(st_mm, 2 * n + 2)
                if n:
                    dve.wait_ge(ret_mm, n)
                dve.tensor_tensor(st_sb[:, :], mid_ps[:, :], T("decay"), ALU.mult).then_inc(st_evac, 1)

            def next_state(n):
                dve.wait_ge(kv_mm, n + 1)
                if n:
                    dve.wait_ge(state_step, RH * n)
                else:
                    dve.wait_ge(state_zeroed, 1)
                if n >= 2:
                    dve.wait_ge(ret_mm, n)
                for h in range(RH):
                    p, hh = h // 2, h % 2
                    r, w = slice(64 * hh, 64 * hh + 64), slice(hh * RV, (hh + 1) * RV)
                    kv = mid_ps[r, p * RV:(p + 1) * RV]
                    if n == 0:
                        ins = dve.tensor_copy(state[r, 0, p, w], kv)
                    else:
                        ins = dve.scalar_tensor_tensor(out=state[r, n % 2, p, w], in0=state[r, (n - 1) % 2, p, w],
                                                       scalar=T("g_chunk")[r, p:p + 1], in1=kv,
                                                       op0=ALU.mult, op1=ALU.add)
                    ins.then_inc(state_step, 1)

            def retention_out(n):
                dve.wait_ge(ret_step, 3 * n + 3)
                if tmp_read[0]:
                    dve.wait_ge(*tmp_read[0])
                dve.tensor_tensor(tmp[:, :].rearrange("p (h d) -> p h d", h=RH),
                                  mid_ps[:, :].rearrange("p (h d) -> p h d", h=RH),
                                  rcoef.rearrange("p (h d) -> p h d", d=1).broadcast_to([P, RH, RV]),
                                  ALU.mult).then_inc(y_ret_psum, 1)
                dve.wait_ge(y_ret_psum, n + 1)
                dve.wait_ge(rgate_done, n + 1)
                half = mix[:, n, ATT_W:2 * ATT_W]
                dve.tensor_tensor(half, half, tmp[:, :], ALU.mult).then_inc(ret_mixed, 1)
                tmp_read[0] = (ret_mixed, n + 1)

            def mix_lo(m):
                for half in range(2):
                    dve.wait_ge(mixhi_done, 2 * m + half + 1)
                    ks, t = slice(KH * half, KH * (half + 1)), slice(m * P, (m + 1) * P)
                    dve.tensor_tensor(xT_lo[:, ks, t], trans_ps[half][:, :].rearrange("p (k t) -> p k t", k=KH),
                                      xT_hi[:, ks, t].bitcast(F32), ALU.subtract).then_inc(mixlo_done, 1)

            def add_residual(i):
                m, n = i // 2, i % 2
                w = slice(n * CW, (n + 1) * CW)
                dve.wait_ge(proj_done, GROUPS + i + 1)
                dve.wait_ge(again_in[m], 16)
                dve.tensor_tensor(h_out[:, m, w], proj_ps[i % 2][:, :], x_again[:, m % 2, w], ALU.add).then_inc(h_added, 1)
                if n == 0:
                    return
                dve.wait_ge(h_step, 3 * m + 3)
                dve.wait_ge(fgain_in, 16)
                for n in range(2):
                    w = slice(n * CW, (n + 1) * CW)
                    dve.scalar_tensor_tensor(out=h_out[:, m, w], in0=h_out[:, m, w], scalar=out_rstd[:, m:m + 1],
                                             in1=fgain[:, w], op0=ALU.mult, op1=ALU.mult).then_inc(h_ready, 1)

            for g in range(GROUPS + OUT_GROUPS):
                for u in splits_at(g):
                    split_lo(u)
                if g >= RET0 + 1 and (g - RET0) % 2 == 1 and (g - RET0) // 2 < MT - 1:
                    next_state((g - RET0) // 2)
                if g >= GROUPS - 1 and (g - GROUPS + 1) % 2 == 0 and (g - GROUPS + 1) // 2 < MT:
                    mix_lo((g - GROUPS + 1) // 2)
                if MT * C_RG <= g < GROUPS:
                    gate(g)
                if g >= GROUPS:
                    add_residual(g - GROUPS)
                if g >= TOPK0:
                    for r in range(PER_SLOT * (g - TOPK0), min(PER_SLOT * (g - TOPK0 + 1), ROUNDS * (MT - 1))):
                        topk_round(r)
                if MT <= g < 2 * MT - 1:
                    index_scores(g - MT + 1)
                s = g - ATT0 - 2
                if 0 <= s < STEPS and s % PAIRS == PAIRS - 1:
                    attention_out(s // PAIRS)
                if 0 <= g - ATT0 < STEPS:
                    masked_max(g - ATT0)
                if RET0 <= g < RET0 + 2 * MT:
                    if (g - RET0) % 2 == 0:
                        decayed((g - RET0) // 2)
                    else:
                        retention_out((g - RET0) // 2)

    return nc


_INS = ["x", "norm_gain", "w_in", "w_out", "final_gain"]


def kernel(**inputs):
    import concourse.bacc as bacc
    from concourse.bass_utils import run_bass_kernel_spmd

    nc = bacc.Bacc("TRN2", target_bir_lowering=False, num_devices=1)
    arrays = {n: np.ascontiguousarray(inputs[n]) for n in _INS}
    arrays["table"] = tables()
    args = [nc.dram_tensor(f"in_{n}", a.shape, mybir.dt.from_np(a.dtype), kind="ExternalInput").ap()
            for n, a in arrays.items()]
    out = nc.dram_tensor("out", (1, SEQ, D_MODEL), F32, kind="ExternalOutput").ap()
    hymba_layer(nc, *args, out)
    r = run_bass_kernel_spmd(nc, [{f"in_{n}": a for n, a in arrays.items()}], core_ids=[0])
    return r.results[0]["out"]
```

```python
from contextlib import ExitStack

import numpy as np

import concourse.bass as bass
from concourse import mybir

F32 = mybir.dt.float32
F32R = mybir.dt.float32r
ALU = mybir.AluOpType
ACT = mybir.ActivationFunctionType

P = 128
SEQ, D_MODEL = 512, 1024
MT = SEQ // P
KT = D_MODEL // P
HEADS, HD = 8, 64
ATT_W = HEADS * HD
IDX_HEADS, IDX_DIM = 4, 64
ROPE_HALF = HD // 4 // 2
ROPE_THETA = 500000.0
TOPK = min(256, SEQ // 4)
RH, RQK, RV = 4, 64, 128
RET_THETA = 10000.0
RET_HALF = RQK // 2
EPS = 1e-6
MASKED = -1e30
TAKEN = -3e38
NEVER = -2e38

IDX_W = IDX_HEADS * IDX_DIM + IDX_DIM + IDX_HEADS
BASE = 4 * ATT_W
CHUNKS = [("idx", BASE, IDX_W), ("q", 0, ATT_W), ("k", ATT_W, ATT_W), ("v", 2 * ATT_W, ATT_W),
          ("ret_qk", BASE + IDX_W, 2 * RH * RQK),
          ("ret_v", BASE + IDX_W + 2 * RH * RQK, RH * RV),
          ("ret_gate", BASE + IDX_W + 2 * RH * RQK + RH * RV, RH * RV),
          ("att_gate", 3 * ATT_W, ATT_W)]
NCH = len(CHUNKS)
CW = 512
KH = KT // 2
UNITS = 2 * NCH + 4
RAW, RING = 2, 4
GROUPS = NCH * MT
OUT_GROUPS = 2 * MT
C_V, C_RQK, C_RV, C_RG, C_AG = 3, 4, 5, 6, 7
ATT0 = MT * C_RQK
PAIRS = HEADS // 2
STEPS = MT * PAIRS
RET0 = MT * C_RG
TOPK0 = 5
ROUNDS = TOPK // 8

TAB = {}
_at = 0
for _n, _w in (("att_cos", MT * ROPE_HALF), ("att_sin", MT * 2 * ROPE_HALF),
               ("ret_cos", MT * RET_HALF), ("ret_sin", MT * 2 * RET_HALF), ("decay", RH * P),
               ("xi", 2 * P), ("zeta", RH), ("g_chunk", 2), ("causal", P)):
    TAB[_n] = (_at, _at + _w)
    _at += _w
TAB_W = _at


def tables():
    t = np.zeros((P, TAB_W), np.float32)

    def put(name, a):
        lo, hi = TAB[name]
        t[:, lo:hi] = np.asarray(a, np.float32).reshape(P, hi - lo)

    def rope(half, theta):
        inv = np.float32(1.0) / (np.float32(theta) ** (np.arange(half, dtype=np.float32) / np.float32(half)))
        ang = (np.arange(SEQ, dtype=np.float32)[:, None] * inv[None, :]).astype(np.float32).astype(np.float64)
        c = np.cos(ang).reshape(MT, P, half).transpose(1, 0, 2)
        s = np.sin(ang).reshape(MT, P, half).transpose(1, 0, 2)
        return c, np.stack([-s, s], axis=2)

    c, s = rope(ROPE_HALF, ROPE_THETA)
    put("att_cos", c), put("att_sin", s)
    c, s = rope(RET_HALF, RET_THETA)
    put("ret_cos", c), put("ret_sin", s)
    log_g = np.log((1.0 - 2.0 ** (-5.0 - np.arange(RH))).astype(np.float32)).astype(np.float64)
    i = np.arange(P, dtype=np.float64)
    diff = i[None, :] - i[:, None]
    decay = np.where(diff[None] >= 0, np.exp(log_g[:, None, None] * np.maximum(diff, 0)), 0.0)
    put("decay", decay.transpose(1, 0, 2) * RQK ** -0.5)
    xi = np.exp(log_g[:, None] * (i + 1.0)[None, :])
    put("xi", np.repeat(xi.reshape(2, 2, P), RQK, axis=1).transpose(1, 0, 2))
    put("zeta", (np.exp(log_g[:, None] * (P - 1.0 - i)[None, :]) * RQK ** -0.5).T)
    put("g_chunk", np.repeat(np.exp(log_g * P).reshape(2, 2), RQK, axis=1).T)
    put("causal", np.where(i[None, :] <= i[:, None], 0.0, MASKED))
    return t


def unit_source(u, w_in, w_out):
    if u < 2 * NCH:
        _, c0, w = CHUNKS[u // 2]
        src = w_in[0]
    else:
        c0, w, src = CW * ((u - 2 * NCH) // 2), CW, w_out[0]
    k0 = KH * (u % 2)
    return src[k0 * P:(k0 + KH) * P, c0:c0 + w].rearrange("(k p) c -> p k c", p=P), w


def splits_at(slot):
    if slot == GROUPS:
        return [UNITS - 2, UNITS - 1]
    if slot < GROUPS and slot % MT == 0:
        return [2 * (slot // MT + 1)]
    if slot < GROUPS and slot % MT == 2:
        return [2 * (slot // MT + 1) + 1]
    return []


def steps_before_mix(m):
    return min(STEPS, GROUPS - 2 + 2 * m - ATT0)


def rounds_at(slot):
    done = 0
    for g in range(TOPK0, slot + 1):
        n = min(4 if g < 14 else 2, ROUNDS * (MT - 1) - done)
        done += n
    return range(done - n, done) if slot >= TOPK0 else range(0)


def transposed(g):
    c = g // MT
    if g < 0 or g >= GROUPS or c not in (0, 1, 2, C_RQK):
        return None
    return g if c < 3 else g - MT


def hymba_layer(nc, x, norm_gain, w_in, w_out, final_gain, table, out):
    with ExitStack() as ctx:
        def sb(name, shape, dt=F32):
            return ctx.enter_context(nc.sbuf_tensor(name, shape, dt))

        def sem(name):
            return ctx.enter_context(nc.semaphore(name))

        tab = sb("tab", [P, TAB_W])
        ident_t = sb("ident_t", [P, P])
        ident = ident_t[:, :]
        xT_hi = sb("xT_hi", [P, KT, SEQ], F32R)
        xT_lo = sb("xT_lo", [P, KT, SEQ], F32R)
        w_raw = sb("w_raw", [P, RAW, KH * CW])
        w_hi = sb("w_hi", [P, RING, KH * CW], F32R)
        w_lo = sb("w_lo", [P, RING, KH * CW], F32R)
        x_qkT = sb("x_qkT", [P, 2 * PAIRS * SEQ])
        x_in = x_qkT[:, :].rearrange("p (m d) -> p m d", m=MT)
        qT = x_qkT[:, 0:PAIRS * SEQ].rearrange("p (a t) -> p a t", a=PAIRS)
        kT = x_qkT[:, PAIRS * SEQ:].rearrange("p (a t) -> p a t", a=PAIRS)
        with nc.sbuf_tensor("idx_stack", [P, IDX_HEADS + 2, SEQ], F32R) as idx_stack:
            idx_q, idx_kh, idx_kl = idx_stack[:, 0:IDX_HEADS, :], idx_stack[:, IDX_HEADS, :], idx_stack[:, IDX_HEADS + 1, :]
        retT = sb("retT", [P, 6, SEQ])
        qrT, krT, qxT = retT[:, 0:2, :], retT[:, 2:4, :], retT[:, 4:6, :]
        v_att = sb("v_att", [P, MT, ATT_W])
        v_ret = sb("v_ret", [P, MT, RH * RV])
        kz = sb("kz", [P, MT, RH * RQK])
        zt = sb("zt", [P, 2, CW])
        w_idx = sb("w_idx", [P, MT, IDX_HEADS])
        keys = [None] + [sb(f"keys{b}", [P, (b + 1) * P]) for b in range(1, MT)]
        top8 = sb("top8", [P, 8])
        work = sb("work", [P, 4, SEQ])
        prob = work[:, 0:2, :]
        probT = work[:, 2:4, :]
        mix = sb("mix", [P, MT, 2 * ATT_W])
        th = sb("th", [P, CW])
        tmp = sb("tmp", [P, CW])
        rope_a, rope_b = th, tmp
        junk = sb("junk", [P, CW])
        st_sb = sb("st_sb", [P, RH * P])
        state = zt[:, :, :].rearrange("p n (a e) -> p n a e", a=2)
        small = sb("small", [P, 128])
        gain_rows = st_sb[0:KT, 0:P]
        gain = small[:, 0:8]
        ssq, rstd, half_rstd = small[:, 8:12], small[:, 12:16], small[:, 16:20]
        row_max = small[:, 20:22]
        neg_max = small[:, 22:24]
        den = small[:, 24:40].rearrange("p (b h) -> p b h", b=2)
        rden, acoef = small[:, 40:48], small[:, 48:56]
        ret_ms, ret_r, rcoef = small[:, 56:60], small[:, 60:64], small[:, 64:68]
        out_ms, out_ms1, out_rstd = small[:, 68:76], small[:, 76:80], small[:, 80:84]
        minus_half, ms_eps = small[:, 84:88], small[:, 88:92]
        x_again = w_raw[:, 0, :].rearrange("p (m d) -> p m d", m=2)
        fgain = w_raw[:, 1, 0:D_MODEL]
        h_out = x_qkT[:, :].rearrange("p (m d) -> p m d", m=MT)

        bank = [ctx.enter_context(nc.psum_tensor(f"bank{i}", [P, 512], F32)) for i in range(8)]
        proj_ps, score_ps, trans_ps, att_ps, mid_ps = bank[0:2], bank[2:4], bank[4:6], bank[6], bank[7]
        idx_ps = bank[2:6]

        tab_in, x_loaded, gain_in = sem("tab_in"), [sem(f"x_in{m}") for m in range(MT)], sem("gain_in")
        raw_in = [sem(f"raw_in{i}") for i in range(RAW)]
        again_in, fgain_in, stored = [sem(f"again_in{i}") for i in range(MT)], sem("fgain_in"), sem("stored")
        ident_zero, ident_done = sem("ident_zero"), sem("ident_done")
        gain_t, gain_ok, xt_done, xhi_done, xlo_done = (sem(n) for n in ("gain_t", "gain_ok", "xt_done", "xhi_done", "xlo_done"))
        warmed, sq_even, sq_odd, minus_half_done, rstd_done, hrstd_done = (sem(n) for n in ("warmed", "sq_even", "sq_odd", "minus_half_done", "rstd_done", "hrstd_done"))
        whi_done, wlo_done, proj_done = sem("whi_done"), sem("wlo_done"), sem("proj_done")
        z_done, w_idx_done = sem("z_done"), sem("w_idx_done")
        rope_step, rope_done, t_done, t_evac, qx_done = (sem(n) for n in ("rope_step", "rope_done", "t_done", "t_evac", "qx_done"))
        idx_lo_done, idx_mm, relu_done, score_step, round_step, mask_done = (sem(n) for n in ("idx_lo_done", "idx_mm", "relu_done", "score_step", "round_step", "mask_done"))
        qk_done, max_done, negmax_done, exp_done = (sem(n) for n in ("qk_done", "max_done", "negmax_done", "exp_done"))
        pt_done, pt_evac, pv_done, att_step, y_att_psum, att_mixed = (sem(n) for n in ("pt_done", "pt_evac", "pv_done", "att_step", "y_att_psum", "att_mixed"))
        tanh_done, rgate_done, agate_psum = (sem(n) for n in ("tanh_done", "rgate_done", "agate_psum"))
        state_zeroed, st_mm, st_evac, kv_mm, state_step, ret_mm, ret_sq, ret_step, y_ret_psum, ret_mixed = (
            sem(n) for n in ("state_zeroed", "st_mm", "st_evac", "kv_mm", "state_step", "ret_mm", "ret_sq", "ret_step", "y_ret_psum", "ret_mixed"))
        mixT_mm, mixhi_done, mixlo_done = sem("mixT_mm"), sem("mixhi_done"), sem("mixlo_done")
        h_added, h_gained, h_sq, h_step, left_ready, right_ready = (
            sem(n) for n in ("h_added", "h_gained", "h_sq", "h_step", "left_ready", "right_ready"))

        def T(name):
            lo, hi = TAB[name]
            return tab[:, lo:hi]

        def x_ps(m, k):
            return bank[2 + 2 * (m % 3) + k // KH][:, (k % KH) * P:(k % KH + 1) * P]

        block = ctx.enter_context(nc.Block())

        def cols(b):
            return (b + 1) * P

        @block.sync
        def _(sp):
            def load_x(m):
                sp.dma_start(x_in[:, m, :], x[0, m * P:(m + 1) * P, :]).then_inc(x_loaded[m], 16)

            load_x(0)
            sp.dma_start(gain_rows, norm_gain[0].rearrange("(k p) -> k p", p=P)).then_inc(gain_in, 16)
            for u in range(UNITS):
                src, w = unit_source(u, w_in, w_out)
                if u >= RAW:
                    sp.wait_ge(wlo_done, u - RAW + 1)
                dst = w_raw[:, u % RAW, :].rearrange("p (k c) -> p k c", k=KH)[:, :, 0:w]
                sp.dma_start(dst, src).then_inc(raw_in[u % RAW], 16)
                if u == 0:
                    load_x(1)
                if u == 1:
                    load_x(2)
                    load_x(3)
                    sp.dma_start(tab[:, :], table).then_inc(tab_in, 16)
            sp.wait_ge(wlo_done, UNITS - 1)
            for m in range(2):
                sp.dma_start(x_again[:, m, :], x[0, m * P:(m + 1) * P, :]).then_inc(again_in[m], 16)
            sp.wait_ge(wlo_done, UNITS)
            sp.dma_start(fgain, final_gain.rearrange("(a d) -> a d", a=1).broadcast_to([P, D_MODEL])).then_inc(fgain_in, 16)
            for m in range(MT):
                if m >= 2:
                    sp.wait_ge(h_gained, 2 * (m - 1))
                    sp.wait_ge(h_sq, 2 * (m - 1))
                    sp.dma_start(x_again[:, m % 2, :], x[0, m * P:(m + 1) * P, :]).then_inc(again_in[m], 16)
            for m in range(MT):
                for n in range(2):
                    sp.wait_ge(right_ready if n else left_ready, m + 1)
                    sp.dma_start(out[0, m * P:(m + 1) * P, n * CW:(n + 1) * CW],
                                 h_out[:, m, n * CW:(n + 1) * CW]).then_inc(stored, 16)
            sp.wait_ge(stored, 16 * 2 * MT)

        @block.tensor
        def _(pe):
            pe.wait_ge(gain_in, 16)
            pe.wait_ge(ident_done, 1)
            pe.transpose(mid_ps[:, 0:KT], gain_rows, ident[0:KT, 0:KT]).then_inc(gain_t, 1)

            def transpose_x(m):
                pe.wait_ge(x_loaded[m], 16)
                for k in range(KT):
                    if m == MT - 1 and k % KH == 0:
                        pe.wait_ge(xlo_done, k + KH)
                    mm = pe.transpose(x_ps(m, k), x_in[:, m, k * P:(k + 1) * P], ident)
                    if k % KH == KH - 1:
                        mm.then_inc(xt_done, 1)

            transpose_x(0)
            transpose_x(1)

            def proj(g, half):
                if g < GROUPS:
                    c, m = g // MT, g % MT
                    u, w = 2 * c + half, CHUNKS[c][2]
                else:
                    m, n = (g - GROUPS) // 2, (g - GROUPS) % 2
                    u, w = 2 * NCH + 2 * n + half, CW
                if half == 0:
                    if 2 <= g < MT * C_RG + 2:
                        pe.wait_ge(z_done, g - 1)
                    elif MT * C_RG + 2 <= g < MT * C_AG + 2:
                        pe.wait_ge(rgate_done, g - 2 - MT * C_RG + 1)
                    elif MT * C_AG + 2 <= g < GROUPS + 2:
                        pe.wait_ge(agate_psum, g - 2 - MT * C_AG + 1)
                    elif g >= GROUPS + 2:
                        pe.wait_ge(h_added, g - 2 - GROUPS + 1)
                    if g < MT:
                        pe.wait_ge(xlo_done, KT * (g + 1))
                    if g >= GROUPS:
                        pe.wait_ge(mixlo_done, 2 * (m + 1))
                pe.wait_ge(wlo_done, u + 1)
                o = proj_ps[g % 2][:, 0:w]
                hi = w_hi[:, u % RING, :].rearrange("p (k c) -> p k c", k=KH)
                lo = w_lo[:, u % RING, :].rearrange("p (k c) -> p k c", k=KH)
                for kk in range(KH):
                    k = KH * half + kk
                    xh, xl = (t[:, k, m * P:(m + 1) * P] for t in (xT_hi, xT_lo))
                    first, last = k == 0, k == KT - 1
                    pe.matmul(o, xh, hi[:, kk, 0:w], start=first, stop=False)
                    pe.matmul(o, xh, lo[:, kk, 0:w], start=False, stop=False)
                    mm = pe.matmul(o, xl, hi[:, kk, 0:w], start=False, stop=last)
                if half == 1:
                    mm.then_inc(proj_done, 1)

            def transpose_group(g):
                i = transposed(g)
                if i is None:
                    return
                pe.wait_ge(rope_done, i + 1)
                if i == 0:
                    pe.wait_ge(xlo_done, 3 * KT)
                if i >= 1:
                    pe.wait_ge(t_evac, i)
                    pe.wait_ge(idx_lo_done, min(i, MT))
                for j in range(3 if g < MT else 4):
                    mm = pe.transpose(mid_ps[:, j * P:(j + 1) * P], zt[:, g % 2, j * P:(j + 1) * P], ident)
                mm.then_inc(t_done, 1)

            def index_logits(b):
                pe.wait_ge(idx_lo_done, b + 1)
                for h in range(IDX_HEADS):
                    n = IDX_HEADS * (b - 1) + h
                    if n >= IDX_HEADS:
                        pe.wait_ge(relu_done, n - IDX_HEADS + 1)
                    else:
                        pe.wait_ge(xlo_done, MT * KT)
                    q, o = idx_q[:, h, b * P:(b + 1) * P], idx_ps[h][:, 0:cols(b)]
                    pe.matmul(o, q, idx_kh[:, 0:cols(b)], start=True, stop=False)
                    pe.matmul(o, q, idx_kl[:, 0:cols(b)], start=False, stop=True).then_inc(idx_mm, 1)

            def values(s):
                b, p = s // PAIRS, s % PAIRS
                if p == 0 and b >= 1:
                    pe.wait_ge(y_att_psum, b)
                for hh in range(2):
                    h = 2 * p + hh
                    pe.wait_ge(pt_evac, 2 * s + hh + 1)
                    for j in range(b + 1):
                        mm = pe.matmul(att_ps[:, h * HD:(h + 1) * HD], probT[:, hh, j * P:(j + 1) * P],
                                       v_att[:, j, h * HD:(h + 1) * HD], start=(j == 0), stop=(j == b))
                mm.then_inc(pv_done, 1)

            def transpose_probs(s):
                b = s // PAIRS
                for hh in range(2):
                    pe.wait_ge(exp_done, 2 * s + hh + 1)
                    if s >= 1:
                        pe.wait_ge(pt_evac, 2 * s + hh - 1)
                    for m in range(MT):
                        if s == steps_before_mix(m):
                            pe.wait_ge(mixlo_done, 2 * m + hh + 1)
                    for j in range(b + 1):
                        mm = pe.transpose(trans_ps[hh][:, j * P:(j + 1) * P], prob[:, hh, j * P:(j + 1) * P], ident)
                    mm.then_inc(pt_done, 1)

            def scores(s):
                b, p = s // PAIRS, s % PAIRS
                pe.wait_ge(t_evac, 3 * MT)
                for hh in range(2):
                    if s == 0:
                        pe.wait_ge(relu_done, IDX_HEADS * (MT - 1))
                    else:
                        pe.wait_ge(max_done, 2 * s + hh - 1)
                    r = slice(64 * hh, 64 * hh + 64)
                    pe.matmul(score_ps[hh][:, 0:cols(b)], qT[r, p, b * P:(b + 1) * P], kT[r, p, 0:cols(b)],
                              start=True, stop=True).then_inc(qk_done, 1)

            def ret_scores(n, hh):
                r = slice(64 * hh, 64 * hh + 64)
                if hh:
                    pe.wait_ge(st_mm, 2 * n + 1)
                else:
                    pe.wait_ge(t_evac, 4 * MT)
                    if n >= 1:
                        pe.wait_ge(y_ret_psum, n)
                for h in (hh, hh + 2):
                    mm = pe.matmul(mid_ps[:, h * P:(h + 1) * P], krT[r, h // 2, n * P:(n + 1) * P],
                                   qrT[r, h // 2, n * P:(n + 1) * P], start=True, stop=True)
                mm.then_inc(st_mm, 1)

            def ret_kv(n):
                pe.wait_ge(st_evac, n + 1)
                for h in range(RH):
                    r = 64 * (h % 2)
                    mm = pe.matmul(mid_ps[r:r + 64, (h // 2) * RV:(h // 2 + 1) * RV],
                                   kz[:, n, h * RQK:(h + 1) * RQK], v_ret[:, n, h * RV:(h + 1) * RV],
                                   start=True, stop=True)
                mm.then_inc(kv_mm, 1)

            def ret_out(n):
                pe.wait_ge(st_evac, n + 1)
                pe.wait_ge(state_step, RH * min(n + 1, MT - 1))
                for p in range(2):
                    if n:
                        pe.matmul(mid_ps[:, 2 * p * RV:2 * (p + 1) * RV], qxT[:, p, n * P:(n + 1) * P],
                                  state[:, (n - 1) % 2, p, :], start=True, stop=False)
                    for h in (2 * p, 2 * p + 1):
                        mm = pe.matmul(mid_ps[:, h * RV:(h + 1) * RV], st_sb[:, h * P:(h + 1) * P],
                                       v_ret[:, n, h * RV:(h + 1) * RV], start=(n == 0), stop=(n == 0 or h % 2 == 1))
                mm.then_inc(ret_mm, 1)

            def transpose_mix(m):
                pe.wait_ge(att_mixed, m + 1)
                pe.wait_ge(ret_mixed, m + 1)
                pe.wait_ge(pt_evac, 2 * steps_before_mix(m))
                for half in range(2):
                    if m >= 1:
                        pe.wait_ge(mixlo_done, 2 * (m - 1) + half + 1)
                    for j in range(KH):
                        e = (KH * half + j) * P
                        mm = pe.transpose(trans_ps[half][:, j * P:(j + 1) * P], mix[:, m, e:e + P], ident)
                    mm.then_inc(mixT_mm, 1)

            for g in range(GROUPS + OUT_GROUPS):
                proj(g, 0)
                if g == 0:
                    pe.wait_ge(gain_ok, 1)
                    transpose_x(2)
                    transpose_x(3)
                if g >= RET0 + 1 and (g - RET0) % 2 == 1 and (g - RET0) // 2 < MT - 1:
                    ret_kv((g - RET0) // 2)
                if g >= GROUPS - 1 and (g - GROUPS + 1) % 2 == 0 and (g - GROUPS + 1) // 2 < MT:
                    transpose_mix((g - GROUPS + 1) // 2)
                proj(g, 1)
                transpose_group(g - 1)
                if MT <= g < 2 * MT - 1:
                    index_logits(g - MT + 1)
                retention = RET0 <= g < RET0 + 2 * MT
                if retention and (g - RET0) % 2 == 0:
                    ret_scores((g - RET0) // 2, 0)
                if 0 <= g - ATT0 - 2 < STEPS:
                    values(g - ATT0 - 2)
                if retention and (g - RET0) % 2 == 0:
                    ret_scores((g - RET0) // 2, 1)
                if 0 <= g - ATT0 - 1 < STEPS:
                    transpose_probs(g - ATT0 - 1)
                if 0 <= g - ATT0 < STEPS:
                    scores(g - ATT0)
                if retention and (g - RET0) % 2:
                    n = (g - RET0) // 2
                    if n == 1:
                        pe.wait_ge(qx_done, MT)
                    ret_out(n)

        @block.scalar
        def _(act):
            def split_hi(u):
                w = unit_source(u, w_in, w_out)[1]
                act.wait_ge(raw_in[u % RAW], 16 * (u // RAW + 1))
                if u >= RING:
                    act.wait_ge(proj_done, MT * (u // 2 - 1))
                s, d = (t.rearrange("p (k c) -> p k c", k=KH)[:, :, 0:w] for t in (w_raw[:, u % RAW, :], w_hi[:, u % RING, :]))
                act.activation(d, s, ACT.Copy).then_inc(whi_done, 1)

            def square_x(m):
                act.wait_ge(x_loaded[m], 16)
                act.activation(mix[:, m, :], x_in[:, m, :], ACT.Square, scale=D_MODEL ** -0.5,
                               accum_out=ssq[:, m:m + 1]).then_inc(sq_even, 1)

            def x_hi(m):
                for k in range(KT):
                    act.wait_ge(xt_done, 2 * m + k // KH + 1)
                    act.activation(xT_hi[:, k, m * P:(m + 1) * P], x_ps(m, k), ACT.Copy,
                                   scale=gain[:, k:k + 1]).then_inc(xhi_done, 1)

            act.wait_ge(ident_done, 1)
            act.activation(junk[:, 0:1], ident[:, 0:1], ACT.Exp).then_inc(warmed, 1)
            act.wait_ge(gain_ok, 1)
            x_hi(0)
            split_hi(0)
            split_hi(1)
            x_hi(1)
            square_x(0)
            square_x(2)
            x_hi(2)

            def project_out(g):
                c, m = g // MT, g % MT
                act.wait_ge(proj_done, g + 1)
                act.wait_ge(hrstd_done, m + 1)
                src = proj_ps[g % 2]
                scale = rstd[:, m:m + 1]
                i = transposed(g)
                if i is not None:
                    if i >= 2:
                        act.wait_ge(t_done, i - 1)
                    w = 5 * IDX_DIM if c == 0 else CW
                    if c == 0:
                        act.activation(w_idx[:, m, :], src[:, w:w + IDX_HEADS], ACT.Copy, scale=scale).then_inc(w_idx_done, 1)
                    act.activation(zt[:, g % 2, 0:w], src[:, 0:w], ACT.Copy, scale=scale).then_inc(z_done, 1)
                elif c in (C_V, C_RV):
                    dst = (v_att if c == C_V else v_ret)[:, m, :]
                    act.activation(dst, src[:, :], ACT.Copy, scale=scale).then_inc(z_done, 1)
                else:
                    i = g - MT * C_RG
                    if i > MT:
                        act.wait_ge(agate_psum, i - MT)
                    elif i:
                        act.wait_ge(rgate_done, i)
                    else:
                        act.wait_ge(rope_done, 4 * MT)
                    act.activation(th[:, :], src[:, :], ACT.Tanh, scale=half_rstd[:, m:m + 1]).then_inc(tanh_done, 1)

            def transposed_out(g):
                i = transposed(g)
                if i is None:
                    return
                c, m = g // MT, g % MT
                t = slice(m * P, (m + 1) * P)
                act.wait_ge(t_done, i + 1)
                if c == 0:
                    for hh in range(2):
                        act.activation(idx_q[0:64, hh::2, t], mid_ps[64 * hh:64 * hh + 64, 0:2 * P].rearrange(
                            "p (a t) -> p a t", a=2), ACT.Copy)
                    act.activation(idx_kh[:, t], mid_ps[:, 2 * P:3 * P], ACT.Copy).then_inc(t_evac, 1)
                    return
                if i == 3 * MT:
                    act.wait_ge(idx_mm, IDX_HEADS * (MT - 1))
                src = mid_ps[:, :].rearrange("p (a t) -> p a t", a=4)
                dst = {1: qT, 2: kT, C_RQK: retT[:, 0:4, :]}[c][:, :, t]
                act.activation(dst, src, ACT.Copy).then_inc(t_evac, 1)

            def relus(b):
                for h in range(IDX_HEADS):
                    n = IDX_HEADS * (b - 1) + h
                    act.wait_ge(idx_mm, n + 1)
                    if b >= 2:
                        act.wait_ge(score_step, 5 * (b - 2) + h + 1)
                    act.activation(work[:, h, 0:cols(b)], idx_ps[h][:, 0:cols(b)], ACT.Relu).then_inc(relu_done, 1)

            def exps(s):
                b, p = s // PAIRS, s % PAIRS
                act.wait_ge(negmax_done, s + 1)
                if p == 0 and b >= 2:
                    act.wait_ge(y_att_psum, b - 1)
                for hh in range(2):
                    pr = prob[:, hh, 0:cols(b)]
                    act.activation(pr, pr, ACT.Exp, bias=neg_max[:, hh:hh + 1], scale=HD ** -0.5,
                                   accum_out=den[:, b % 2, 2 * p + hh:2 * p + hh + 1]).then_inc(exp_done, 1)

            def probT_out(s):
                b = s // PAIRS
                for hh in range(2):
                    act.wait_ge(pt_done, 2 * s + hh + 1)
                    if s >= 1:
                        act.wait_ge(pv_done, s)
                    elif hh == 0:
                        act.wait_ge(score_step, 5 * (MT - 1))
                    act.activation(probT[:, hh, 0:cols(b)], trans_ps[hh][:, 0:cols(b)], ACT.Copy).then_inc(pt_evac, 1)

            def ret_squares(n):
                act.wait_ge(ret_mm, n + 1)
                if n == 0:
                    act.wait_ge(warmed, 1)
                for h in range(RH):
                    if h == 0 and n:
                        act.wait_ge(ret_step, 3 * n)
                        act.wait_ge(ret_sq, RH * n)
                    act.activation(junk[:, h * RV:(h + 1) * RV], mid_ps[:, h * RV:(h + 1) * RV], ACT.Square, scale=RV ** -0.5,
                                   accum_out=ret_ms[:, h:h + 1]).then_inc(ret_sq, 1)

            def mix_hi(m):
                act.wait_ge(proj_done, GROUPS - MT + m + 1)
                for half in range(2):
                    act.wait_ge(mixT_mm, 2 * m + half + 1)
                    act.activation(xT_hi[:, KH * half:KH * (half + 1), m * P:(m + 1) * P],
                                   trans_ps[half][:, :].rearrange("p (k t) -> p k t", k=KH), ACT.Copy).then_inc(mixhi_done, 1)

            for g in range(GROUPS + OUT_GROUPS):
                if g:
                    for u in splits_at(g):
                        split_hi(u)
                if g >= GROUPS - 1 and (g - GROUPS + 1) % 2 == 0 and (g - GROUPS + 1) // 2 < MT:
                    mix_hi((g - GROUPS + 1) // 2)
                if g < GROUPS:
                    project_out(g)
                if g == 0:
                    x_hi(3)
                    split_hi(2)
                transposed_out(g - 1)
                if MT <= g < 2 * MT - 1:
                    relus(g - MT + 1)
                if 0 <= g - ATT0 - 1 < STEPS:
                    probT_out(g - ATT0 - 1)
                if 0 <= g - ATT0 < STEPS:
                    exps(g - ATT0)
                if RET0 <= g < RET0 + 2 * MT and (g - RET0) % 2 == 1:
                    ret_squares((g - RET0) // 2)
                if g >= GROUPS:
                    i = g - GROUPS
                    act.wait_ge(h_added, i + 1)
                    if i:
                        act.wait_ge(h_sq, i)
                    else:
                        act.wait_ge(ret_sq, RH * MT)
                    act.activation(junk[:, :], x_again[:, (i // 2) % 2, (i % 2) * CW:(i % 2 + 1) * CW], ACT.Square,
                                   scale=D_MODEL ** -0.5, accum_out=out_ms[:, i:i + 1]).then_inc(h_sq, 1)
                    if i % 2:
                        m = i // 2
                        right = h_out[:, m, CW:2 * CW]
                        act.wait_ge(h_gained, i + 1)
                        act.wait_ge(h_step, 2 * m + 2)
                        act.activation(right, right, ACT.Copy, scale=out_rstd[:, m:m + 1]).then_inc(right_ready, 1)

        @block.gpsimd
        def _(pool):
            step = 0

            def xi_times_q(m):
                t = slice(m * P, (m + 1) * P)
                pool.wait_ge(t_evac, 3 * MT + m + 1)
                pool.tensor_tensor(qxT[:, :, t], qrT[:, :, t], T("xi").rearrange("p (a t) -> p a t", a=2),
                                   ALU.mult).then_inc(qx_done, 1)

            def chain(ins):
                nonlocal step
                step += 1
                ins.then_inc(rope_step, 1)
                return step

            def rsqrt(out, ms, eps_at, done, count, more=None):
                n = ms.shape[1]
                if more is None:
                    pool.tensor_scalar(eps_at, ms, EPS, None, ALU.add).then_inc(done, 1)
                else:
                    pool.tensor_scalar(eps_at, ms, more, EPS, ALU.add, ALU.add).then_inc(done, 1)
                pool.wait_ge(done, count + 1)
                pool.tensor_tensor(out, eps_at, minus_half[:, 0:n], ALU.pow).then_inc(done, 1)
                pool.wait_ge(done, count + 2)

            pool.memset(ident, 0.0).then_inc(ident_zero, 1)
            pool.wait_ge(ident_zero, 1)
            pool.affine_select(out=ident, in_=ident, compare_op=ALU.not_equal, fill=1.0, base=0,
                               pattern=[[-1, P]], channel_multiplier=1).then_inc(ident_done, 1)
            pool.memset(minus_half, -0.5).then_inc(minus_half_done, 1)
            pool.wait_ge(minus_half_done, 1)

            def x_rstd(m):
                pool.wait_ge(sq_odd if m % 2 else sq_even, m // 2 + 1)
                c = slice(m, m + 1)
                rsqrt(rstd[:, c], ssq[:, c], ms_eps[:, c], rstd_done, 2 * m)
                pool.tensor_scalar(half_rstd[:, c], rstd[:, c], 0.5, None, ALU.mult).then_inc(hrstd_done, 1)

            for g in range(GROUPS):
                i = transposed(g)
                if i is None:
                    continue
                c, m = g // MT, g % MT
                if c == 0:
                    x_rstd(m)
                ret = c == C_RQK
                heads = 5 if c == 0 else 8
                half = RET_HALF if ret else ROPE_HALF
                z4 = zt[:, g % 2, 0:heads * HD].rearrange("p (h d) -> p h d", h=heads)
                z = z4[:, :, 0:2 * half].rearrange("p h (s e) -> p h s e", s=2)
                ta = rope_a[:, 0:heads * 2 * half].rearrange("p (h s e) -> p h s e", h=heads, s=2)
                tb = rope_b[:, 0:heads * 2 * half].rearrange("p (h s e) -> p h s e", h=heads, s=2)
                cos = T("ret_cos" if ret else "att_cos")[:, m * half:(m + 1) * half]
                sin = T("ret_sin" if ret else "att_sin")[:, 2 * m * half:2 * (m + 1) * half]
                cos = cos.rearrange("p (h e) -> p h e", h=1).broadcast_to([P, heads, half])
                sin = sin.rearrange("p (h s e) -> p h s e", h=1, s=2)
                pool.wait_ge(tab_in, 16)
                zg = g + 1
                pool.wait_ge(z_done, zg)
                pool.wait_ge(rope_done, i) if i else None
                for s in range(2):
                    chain(pool.tensor_tensor(ta[:, :, s, :], z[:, :, s, :], cos, ALU.mult))
                    last = chain(pool.tensor_tensor(tb[:, :, s, :], z[:, :, 1 - s, :],
                                                    sin[:, :, s, :].broadcast_to([P, heads, half]), ALU.mult))
                pool.wait_ge(rope_step, last)
                add = pool.tensor_tensor(z, ta, tb, ALU.add)
                if c in (1, 2):
                    add.then_inc(rope_done, 1)
                    continue
                last = chain(add)
                pool.wait_ge(rope_step, last)
                if c == 0:
                    pool.tensor_copy(zt[:, g % 2, 5 * HD:6 * HD], zt[:, g % 2, 4 * HD:5 * HD]).then_inc(rope_done, 1)
                else:
                    pool.tensor_tensor(kz[:, m, :].rearrange("p (h d) -> p h d", h=RH), z4[:, RH:2 * RH, :],
                                       T("zeta").rearrange("p (h d) -> p h d", d=1).broadcast_to([P, RH, RQK]),
                                       ALU.mult).then_inc(rope_done, 1)
                    if m:
                        xi_times_q(m - 1)
            xi_times_q(MT - 1)
            pool.wait_ge(t_done, 4 * MT)
            pool.memset(zt[:, :, :], 0.0).then_inc(state_zeroed, 1)

            for n in range(MT):
                pool.wait_ge(ret_sq, RH * (n + 1))
                rsqrt(ret_r, ret_ms, ms_eps, ret_step, 3 * n)
                if n:
                    pool.wait_ge(y_ret_psum, n)
                pool.tensor_scalar(rcoef, ret_r, half_rstd[:, n:n + 1], None, ALU.mult).then_inc(ret_step, 1)
                pool.wait_ge(ret_step, 3 * n + 3)
            for m in range(MT):
                pool.wait_ge(h_sq, 2 * m + 2)
                rsqrt(out_rstd[:, m:m + 1], out_ms[:, 2 * m:2 * m + 1], out_ms1[:, m:m + 1], h_step, 2 * m,
                      out_ms[:, 2 * m + 1:2 * m + 2])

        @block.vector
        def _(dve):
            def split_lo(u):
                w = unit_source(u, w_in, w_out)[1]
                dve.wait_ge(whi_done, u + 1)
                s, h, d = (t.rearrange("p (k c) -> p k c", k=KH)[:, :, 0:w]
                           for t in (w_raw[:, u % RAW, :], w_hi[:, u % RING, :].bitcast(F32), w_lo[:, u % RING, :]))
                dve.tensor_tensor(d, s, h, ALU.subtract).then_inc(wlo_done, 1)

            dve.wait_ge(gain_t, 1)
            dve.tensor_copy(gain, mid_ps[:, 0:KT]).then_inc(gain_ok, 1)
            dve.wait_ge(gain_ok, 1)
            def x_lo(m):
                for k in range(KT):
                    dve.wait_ge(xhi_done, KT * m + KH * (k // KH + 1))
                    t = slice(m * P, (m + 1) * P)
                    dve.scalar_tensor_tensor(out=xT_lo[:, k, t], in0=x_ps(m, k), scalar=gain[:, k:k + 1],
                                             in1=xT_hi[:, k, t].bitcast(F32), op0=ALU.mult,
                                             op1=ALU.subtract).then_inc(xlo_done, 1)

            def square_x(m):
                dve.wait_ge(x_loaded[m], 16)
                dve.tensor_tensor_reduce(out=mix[:, m, :], in0=x_in[:, m, :], in1=x_in[:, m, :], scale=1.0 / D_MODEL,
                                         scalar=0.0, op0=ALU.mult, op1=ALU.add, accum_out=ssq[:, m:m + 1]).then_inc(sq_odd, 1)

            x_lo(0)
            split_lo(0)
            split_lo(1)
            x_lo(1)
            square_x(1)
            x_lo(2)
            square_x(3)
            x_lo(3)

            def index_lo(m):
                t = slice(m * P, (m + 1) * P)
                dve.wait_ge(t_evac, m + 1)
                for hh in range(2):
                    dve.tensor_tensor(idx_q[64:128, hh::2, t], mid_ps[64 * hh:64 * hh + 64, 0:2 * P].rearrange(
                        "p (a t) -> p a t", a=2), idx_q[0:64, hh::2, t].bitcast(F32), ALU.subtract)
                dve.tensor_tensor(idx_kl[:, t], mid_ps[:, 2 * P:3 * P], idx_kh[:, t].bitcast(F32),
                                  ALU.subtract).then_inc(idx_lo_done, 1)

            def index_scores(b):
                dve.wait_ge(w_idx_done, b + 1)
                for h in range(IDX_HEADS):
                    dve.wait_ge(relu_done, IDX_HEADS * (b - 1) + h + 1)
                    src, w = work[:, h, 0:cols(b)], w_idx[:, b, h:h + 1]
                    if h == 0:
                        ins = dve.tensor_scalar(keys[b][:, :], src, w, None, ALU.mult)
                    else:
                        dve.wait_ge(score_step, 5 * (b - 1) + h)
                        ins = dve.scalar_tensor_tensor(out=keys[b][:, :], in0=src, scalar=w, in1=keys[b][:, :],
                                                       op0=ALU.mult, op1=ALU.add)
                    ins.then_inc(score_step, 1)
                dve.wait_ge(score_step, 5 * (b - 1) + 4)
                diag = keys[b][:, b * P:(b + 1) * P]
                dve.tensor_tensor(diag, diag, T("causal"), ALU.add).then_inc(score_step, 1)

            def topk_round(r):
                b = 1 + r // ROUNDS
                dve.wait_ge(round_step, 2 * r) if r else None
                dve.wait_ge(score_step, 5 * b)
                dve.max(top8[:, :], keys[b][:, :]).then_inc(round_step, 1)
                dve.wait_ge(round_step, 2 * r + 1)
                dve.match_replace(keys[b][:, :], top8[:, :], keys[b][:, :], TAKEN).then_inc(round_step, 1)
                if r % ROUNDS == ROUNDS - 1:
                    dve.wait_ge(round_step, 2 * r + 2)
                    dve.tensor_scalar(keys[b][:, :], keys[b][:, :], NEVER, MASKED, ALU.is_gt, ALU.mult).then_inc(mask_done, 1)

            def masked_max(s):
                b = s // PAIRS
                dve.wait_ge(mask_done, b) if b else None
                if s:
                    dve.wait_ge(negmax_done, s)
                    dve.wait_ge(exp_done, 2 * s)
                for hh in range(2):
                    dve.wait_ge(qk_done, 2 * s + hh + 1)
                    if s:
                        dve.wait_ge(pt_done, 2 * s + hh - 1)
                    if b == 0:
                        mask, o = T("causal"), prob[:, hh, 0:P]
                    else:
                        mask, o = keys[b][:, :], prob[:, hh, 0:cols(b)]
                    dve.tensor_tensor_reduce(out=o, in0=score_ps[hh][:, 0:cols(b)], in1=mask, scale=1.0, scalar=TAKEN,
                                             op0=ALU.add, op1=ALU.max, accum_out=row_max[:, hh:hh + 1]).then_inc(max_done, 1)
                dve.wait_ge(max_done, 2 * s + 2)
                dve.tensor_scalar(neg_max, row_max, -(HD ** -0.5), None, ALU.mult).then_inc(negmax_done, 1)

            tmp_read = [None]

            def gate(g):
                i = g - MT * C_RG
                m, ret = i % MT, i < MT
                dve.wait_ge(tanh_done, i + 1)
                w = slice(ATT_W, 2 * ATT_W) if ret else slice(0, ATT_W)
                straight = ret or m == MT - 1
                if not straight and tmp_read[0]:
                    dve.wait_ge(*tmp_read[0])
                dst = mix[:, m, w] if straight else tmp[:, :]
                dve.scalar_tensor_tensor(out=dst, in0=th[:, :], scalar=1.0, in1=proj_ps[g % 2][:, :], op0=ALU.add,
                                         op1=ALU.mult).then_inc(rgate_done if ret else agate_psum, 1)
                if not straight:
                    dve.wait_ge(agate_psum, m + 1)
                    dve.wait_ge(y_att_psum, m + 1)
                    dve.tensor_tensor(mix[:, m, w], mix[:, m, w], tmp[:, :], ALU.mult).then_inc(att_mixed, 1)
                    tmp_read[0] = (att_mixed, m + 1)

            def attention_out(b):
                dve.wait_ge(pv_done, PAIRS * (b + 1))
                dve.wait_ge(exp_done, 2 * PAIRS * (b + 1))
                if b:
                    dve.wait_ge(y_att_psum, b)
                dve.reciprocal(rden, den[:, b % 2, :]).then_inc(att_step, 1)
                dve.wait_ge(att_step, 2 * b + 1)
                dve.tensor_scalar(acoef, rden, half_rstd[:, b:b + 1], None, ALU.mult).then_inc(att_step, 1)
                dve.wait_ge(att_step, 2 * b + 2)
                co = acoef.rearrange("p (h d) -> p h d", d=1).broadcast_to([P, HEADS, HD])
                src = att_ps[:, :].rearrange("p (h d) -> p h d", h=HEADS)
                half = mix[:, b, 0:ATT_W]
                if b < MT - 1:
                    dve.tensor_tensor(half.rearrange("p (h d) -> p h d", h=HEADS), src, co, ALU.mult).then_inc(y_att_psum, 1)
                else:
                    dve.wait_ge(*tmp_read[0])
                    dve.tensor_tensor(tmp[:, :].rearrange("p (h d) -> p h d", h=HEADS), src, co, ALU.mult).then_inc(y_att_psum, 1)
                    dve.wait_ge(y_att_psum, b + 1)
                    dve.wait_ge(agate_psum, MT)
                    dve.tensor_tensor(half, half, tmp[:, :], ALU.mult).then_inc(att_mixed, 1)
                    tmp_read[0] = (att_mixed, MT)

            def decayed(n):
                dve.wait_ge(st_mm, 2 * n + 2)
                if n:
                    dve.wait_ge(ret_mm, n)
                dve.tensor_tensor(st_sb[:, :], mid_ps[:, :], T("decay"), ALU.mult).then_inc(st_evac, 1)

            def next_state(n):
                dve.wait_ge(kv_mm, n + 1)
                if n:
                    dve.wait_ge(state_step, RH * n)
                else:
                    dve.wait_ge(state_zeroed, 1)
                if n >= 2:
                    dve.wait_ge(ret_mm, n)
                for h in range(RH):
                    p, hh = h // 2, h % 2
                    r, w = slice(64 * hh, 64 * hh + 64), slice(hh * RV, (hh + 1) * RV)
                    kv = mid_ps[r, p * RV:(p + 1) * RV]
                    if n == 0:
                        ins = dve.tensor_copy(state[r, 0, p, w], kv)
                    else:
                        ins = dve.scalar_tensor_tensor(out=state[r, n % 2, p, w], in0=state[r, (n - 1) % 2, p, w],
                                                       scalar=T("g_chunk")[r, p:p + 1], in1=kv,
                                                       op0=ALU.mult, op1=ALU.add)
                    ins.then_inc(state_step, 1)

            def retention_out(n):
                dve.wait_ge(ret_step, 3 * n + 3)
                if tmp_read[0]:
                    dve.wait_ge(*tmp_read[0])
                dve.tensor_tensor(tmp[:, :].rearrange("p (h d) -> p h d", h=RH),
                                  mid_ps[:, :].rearrange("p (h d) -> p h d", h=RH),
                                  rcoef.rearrange("p (h d) -> p h d", d=1).broadcast_to([P, RH, RV]),
                                  ALU.mult).then_inc(y_ret_psum, 1)
                dve.wait_ge(y_ret_psum, n + 1)
                dve.wait_ge(rgate_done, n + 1)
                half = mix[:, n, ATT_W:2 * ATT_W]
                dve.tensor_tensor(half, half, tmp[:, :], ALU.mult).then_inc(ret_mixed, 1)
                tmp_read[0] = (ret_mixed, n + 1)

            def mix_lo(m):
                for half in range(2):
                    dve.wait_ge(mixhi_done, 2 * m + half + 1)
                    ks, t = slice(KH * half, KH * (half + 1)), slice(m * P, (m + 1) * P)
                    dve.tensor_tensor(xT_lo[:, ks, t], trans_ps[half][:, :].rearrange("p (k t) -> p k t", k=KH),
                                      xT_hi[:, ks, t].bitcast(F32), ALU.subtract).then_inc(mixlo_done, 1)

            def add_residual(i):
                m, n = i // 2, i % 2
                w = slice(n * CW, (n + 1) * CW)
                h = x_again[:, m % 2, w]
                dve.wait_ge(proj_done, GROUPS + i + 1)
                dve.wait_ge(again_in[m], 16)
                dve.tensor_tensor(h, proj_ps[i % 2][:, :], h, ALU.add).then_inc(h_added, 1)
                dve.wait_ge(h_added, i + 1)
                dve.wait_ge(fgain_in, 16)
                dve.tensor_tensor(h_out[:, m, w], h, fgain[:, w], ALU.mult).then_inc(h_gained, 1)

            def normalise(m):
                dve.wait_ge(h_step, 2 * m + 2)
                w = slice(0, CW)
                dve.tensor_scalar(h_out[:, m, w], h_out[:, m, w], out_rstd[:, m:m + 1], None, ALU.mult).then_inc(left_ready, 1)

            for g in range(GROUPS + OUT_GROUPS):
                for u in splits_at(g):
                    split_lo(u)
                if g >= RET0 + 1 and (g - RET0) % 2 == 1 and (g - RET0) // 2 < MT - 1:
                    next_state((g - RET0) // 2)
                if g >= GROUPS - 1 and (g - GROUPS + 1) % 2 == 0 and (g - GROUPS + 1) // 2 < MT:
                    mix_lo((g - GROUPS + 1) // 2)
                if MT * C_RG <= g < GROUPS:
                    gate(g)
                if g >= GROUPS:
                    add_residual(g - GROUPS)
                    if g % 2:
                        normalise((g - GROUPS) // 2)
                if 1 <= g <= MT:
                    index_lo(g - 1)
                if MT <= g < 2 * MT - 1:
                    index_scores(g - MT + 1)
                s = g - ATT0 - 2
                if 0 <= s < STEPS and s % PAIRS == PAIRS - 1:
                    attention_out(s // PAIRS)
                if 0 <= g - ATT0 < STEPS:
                    masked_max(g - ATT0)
                if RET0 <= g < RET0 + 2 * MT:
                    if (g - RET0) % 2 == 0:
                        decayed((g - RET0) // 2)
                    else:
                        retention_out((g - RET0) // 2)
                for r in rounds_at(g):
                    topk_round(r)

    return nc


_INS = ["x", "norm_gain", "w_in", "w_out", "final_gain"]


def kernel(**inputs):
    import concourse.bacc as bacc
    from concourse.bass_utils import run_bass_kernel_spmd

    nc = bacc.Bacc("TRN2", target_bir_lowering=False, num_devices=1)
    arrays = {n: np.ascontiguousarray(inputs[n]) for n in _INS}
    arrays["table"] = tables()
    args = [nc.dram_tensor(f"in_{n}", a.shape, mybir.dt.from_np(a.dtype), kind="ExternalInput").ap()
            for n, a in arrays.items()]
    out = nc.dram_tensor("out", (1, SEQ, D_MODEL), F32, kind="ExternalOutput").ap()
    hymba_layer(nc, *args, out)
    r = run_bass_kernel_spmd(nc, [{f"in_{n}": a for n, a in arrays.items()}], core_ids=[0])
    return r.results[0]["out"]
```

```python
from contextlib import ExitStack

import numpy as np

import concourse.bass as bass
from concourse import mybir

F32 = mybir.dt.float32
F32R = mybir.dt.float32r
ALU = mybir.AluOpType
ACT = mybir.ActivationFunctionType

P = 128
SEQ, D_MODEL = 512, 1024
MT = SEQ // P
KT = D_MODEL // P
HEADS, HD = 8, 64
ATT_W = HEADS * HD
IDX_HEADS, IDX_DIM = 4, 64
ROPE_HALF = HD // 4 // 2
ROPE_THETA = 500000.0
TOPK = min(256, SEQ // 4)
RH, RQK, RV = 4, 64, 128
RET_THETA = 10000.0
RET_HALF = RQK // 2
EPS = 1e-6
MASKED = -1e30
TAKEN = -3e38
NEVER = -2e38

IDX_W = IDX_HEADS * IDX_DIM + IDX_DIM + IDX_HEADS
BASE = 4 * ATT_W
CHUNKS = [("idx", BASE, IDX_W), ("q", 0, ATT_W), ("k", ATT_W, ATT_W), ("v", 2 * ATT_W, ATT_W),
          ("ret_qk", BASE + IDX_W, 2 * RH * RQK),
          ("ret_v", BASE + IDX_W + 2 * RH * RQK, RH * RV),
          ("ret_gate", BASE + IDX_W + 2 * RH * RQK + RH * RV, RH * RV),
          ("att_gate", 3 * ATT_W, ATT_W)]
NCH = len(CHUNKS)
CW = 512
OUT_CH = D_MODEL // CW
KH = KT // 2
KQ = 2
QS = KT // KQ
UNITS = QS * (NCH + OUT_CH)
RAW, RING = 3, 6
GROUPS = NCH * MT
OUT_PIECES = [(m, n * CW, CW) for n in range(OUT_CH) for m in range(MT)]
OUT_PIECES[-1:] = [(MT - 1, D_MODEL - CW + w, CW // 2) for w in (0, CW // 2)]
OUT_GROUPS = len(OUT_PIECES)
LEFT = 5 * P
C_V, C_RQK, C_RV, C_RG, C_AG = 3, 4, 5, 6, 7
ATT0 = MT * C_RQK
PAIRS = HEADS // 2
STEPS = MT * PAIRS
RET0 = MT * C_RG
TOPK0 = 5
ROUNDS = TOPK // 8
WARM_UP = 7

TAB_WIDTHS = [("att_cos", MT * ROPE_HALF), ("att_sin", MT * 2 * ROPE_HALF),
              ("ret_cos", MT * RET_HALF), ("ret_sin", MT * 2 * RET_HALF), ("decay", RH * P),
              ("xi", 2 * P), ("zeta", RH), ("g_chunk", 2), ("causal", P)]
TAB, TAB_W = {}, 0
for name, width in TAB_WIDTHS:
    TAB[name] = (TAB_W, TAB_W + width)
    TAB_W += width


def tables():
    t = np.zeros((P, TAB_W), np.float32)

    def put(name, a):
        lo, hi = TAB[name]
        t[:, lo:hi] = np.asarray(a, np.float32).reshape(P, hi - lo)

    def rope(half, theta):
        inv = np.float32(1.0) / (np.float32(theta) ** (np.arange(half, dtype=np.float32) / np.float32(half)))
        ang = (np.arange(SEQ, dtype=np.float32)[:, None] * inv[None, :]).astype(np.float32).astype(np.float64)
        c = np.cos(ang).reshape(MT, P, half).transpose(1, 0, 2)
        s = np.sin(ang).reshape(MT, P, half).transpose(1, 0, 2)
        return c, np.stack([-s, s], axis=2)

    c, s = rope(ROPE_HALF, ROPE_THETA)
    put("att_cos", c), put("att_sin", s)
    c, s = rope(RET_HALF, RET_THETA)
    put("ret_cos", c), put("ret_sin", s)
    log_g = np.log((1.0 - 2.0 ** (-5.0 - np.arange(RH))).astype(np.float32)).astype(np.float64)
    i = np.arange(P, dtype=np.float64)
    diff = i[None, :] - i[:, None]
    decay = np.where(diff[None] >= 0, np.exp(log_g[:, None, None] * np.maximum(diff, 0)), 0.0)
    put("decay", decay.transpose(1, 0, 2) * RQK ** -0.5)
    xi = np.exp(log_g[:, None] * (i + 1.0)[None, :])
    put("xi", np.repeat(xi.reshape(2, 2, P), RQK, axis=1).transpose(1, 0, 2))
    put("zeta", (np.exp(log_g[:, None] * (P - 1.0 - i)[None, :]) * RQK ** -0.5).T)
    put("g_chunk", np.repeat(np.exp(log_g * P).reshape(2, 2), RQK, axis=1).T)
    put("causal", np.where(i[None, :] <= i[:, None], 0.0, MASKED))
    return t


def unit_source(u, w_in, w_out):
    c = u // QS
    if c < NCH:
        _, c0, w = CHUNKS[c]
        src = w_in[0]
    else:
        c0, w, src = CW * (c - NCH), CW, w_out[0]
    k0 = KQ * (u % QS)
    return src[k0 * P:(k0 + KQ) * P, c0:c0 + w].rearrange("(k p) c -> p k c", p=P), w


def splits_at(slot, place):
    u = QS * (slot // MT + 1)
    if slot < MT:
        units = {(2, "middle"): [u, u + 1], (3, "middle"): [u + 2, u + 3]}
    else:
        units = {(0, "start"): [u], (1, "start"): [u + 1], (3, "start"): [u + 2, u + 3]}
    return [x for x in units.get((slot % MT, place), []) if x < UNITS]


def steps_before_mix(m):
    return min(STEPS, GROUPS - 2 + m - ATT0)


def block_split_at(slot):
    if slot == ATT0 - 3:
        return 0
    s = slot + 1 - ATT0
    return s // PAIRS if 0 < s < STEPS and s % PAIRS == 0 else None


def rounds_at(slot):
    done = 0
    for g in range(TOPK0, slot + 1):
        n = min(4 if g <= 8 else 3 if g <= 12 else 2, ROUNDS * (MT - 1) - done)
        done += n
    return range(done - n, done) if slot >= TOPK0 else range(0)


def transposed(g):
    c = g // MT
    if g < 0 or g >= GROUPS or c not in (0, 1, 2, C_RQK):
        return None
    return g if c < 3 else g - MT


def hymba_layer(nc, x, norm_gain, w_in, w_out, final_gain, table, out):
    with ExitStack() as ctx:
        def sb(name, shape, dt=F32):
            return ctx.enter_context(nc.sbuf_tensor(name, shape, dt))

        def sem(name):
            return ctx.enter_context(nc.semaphore(name))

        tab = sb("tab", [P, TAB_W])
        ident_t = sb("ident_t", [P, P])
        ident = ident_t[:, :]
        xT_hi = sb("xT_hi", [P, KT, SEQ], F32R)
        xT_lo = sb("xT_lo", [P, KT, SEQ], F32R)
        w_raw = sb("w_raw", [P, RAW, KQ * CW])
        w_hi = sb("w_hi", [P, RING, KQ * CW], F32R)
        w_lo = sb("w_lo", [P, RING, KQ * CW], F32R)
        with nc.sbuf_tensor("k_stack", [P, HEADS, SEQ], F32R) as k_stack:
            pass
        x_h = sb("x_h", [P, MT, D_MODEL])
        x_in, h_out = x_h, x_h
        qT = sb("qT", [P, PAIRS, SEQ])
        q_hl = sb("q_hl", [P, HEADS, P], F32R)
        q_lh = sb("q_lh", [P, HEADS, P], F32R)
        with nc.sbuf_tensor("idx_stack", [P, IDX_HEADS + 2, SEQ], F32R) as idx_stack:
            idx_q, idx_kh, idx_kl = idx_stack[:, 0:IDX_HEADS, :], idx_stack[:, IDX_HEADS, :], idx_stack[:, IDX_HEADS + 1, :]
        retT = sb("retT", [P, 6, SEQ])
        qrT, krT, qxT = retT[:, 0:2, :], retT[:, 2:4, :], retT[:, 4:6, :]
        v_att = sb("v_att", [P, MT, ATT_W])
        v_ret = sb("v_ret", [P, MT, RH * RV])
        kz = sb("kz", [P, MT, RH * RQK])
        zt = sb("zt", [P, 2, CW])
        w_idx = sb("w_idx", [P, MT, IDX_HEADS])
        keys = [None] + [sb(f"keys{b}", [P, (b + 1) * P]) for b in range(1, MT)]
        top8 = sb("top8", [P, 8])
        work = sb("work", [P, 4, SEQ])
        prob = work[:, 0:2, :]
        probT = work[:, 2:4, :]
        mix = sb("mix", [P, MT, 2 * ATT_W])
        th = sb("th", [P, CW])
        tmp = sb("tmp", [P, CW])
        rope_a, rope_b = th, tmp
        junk = sb("junk", [P, CW])
        st_sb = sb("st_sb", [P, RH * P])
        state = zt[:, :, :].rearrange("p n (a e) -> p n a e", a=2)
        small = sb("small", [P, 128])
        gain_rows = st_sb[0:KT, 0:P]
        gain = small[:, 0:8]
        ssq, rstd, half_rstd = small[:, 8:12], small[:, 12:16], small[:, 16:20]
        row_max = small[:, 20:22]
        neg_max = small[:, 22:24]
        den = small[:, 24:40].rearrange("p (b h) -> p b h", b=2)
        rden, acoef = small[:, 40:48], small[:, 48:56]
        ret_ms, ret_r, rcoef = small[:, 56:60], small[:, 60:64], small[:, 64:68]
        out_ms, out_ms1, out_rstd = small[:, 92:92 + OUT_GROUPS], small[:, 76:80], small[:, 80:84]
        minus_half, ms_eps = small[:, 84:88], small[:, 88:92]
        x_again = retT[:, 0:4, :]
        fgain = retT[:, 4:6, :].rearrange("p a c -> p (a c)")

        bank = [ctx.enter_context(nc.psum_tensor(f"bank{i}", [P, 512], F32)) for i in range(8)]
        proj_ps, score_ps, trans_ps, att_ps, mid_ps = bank[0:2], bank[2:4], bank[4:6], bank[6], bank[7]
        idx_ps = bank[2:6]

        def sems(names):
            return [sem(n) for n in names.split()]

        x0_left, tab_in, gain_in, fgain_in, left_stored, right_stored = sems(
            "x0_left tab_in gain_in fgain_in left_stored right_stored")
        x_loaded = [sem(f"x_in{m}") for m in range(MT)]
        raw_in = [sem(f"raw_in{i}") for i in range(RAW)]
        again_in = [sem(f"again_in{i}") for i in range(4)]
        warm_up_zero, ident_zero, ident_done, warmed, minus_half_done = sems(
            "warm_up_zero ident_zero ident_done warmed minus_half_done")
        gain_t, gain_ok, xt_done, xhi_done, xlo_done = sems("gain_t gain_ok xt_done xhi_done xlo_done")
        sq_even, sq_odd, rstd_done, hrstd_done = sems("sq_even sq_odd rstd_done hrstd_done")
        whi_done, wlo_done, w_used, proj_done, z_done, w_idx_done = sems(
            "whi_done wlo_done w_used proj_done z_done w_idx_done")
        rope_step, rope_done, t_done, t_evac, qx_done = sems("rope_step rope_done t_done t_evac qx_done")
        idx_lo_done, idx_mm, relu_done, score_step, round_step, mask_done = sems(
            "idx_lo_done idx_mm relu_done score_step round_step mask_done")
        klo_done, q_hi_done, q_lo_done, qk_done, max_done, negmax_done, exp_done = sems(
            "klo_done q_hi_done q_lo_done qk_done max_done negmax_done exp_done")
        pt_done, pt_evac, pv_done, att_step, y_att_psum, att_mixed = sems(
            "pt_done pt_evac pv_done att_step y_att_psum att_mixed")
        tanh_done, rgate_done, agate_psum = sems("tanh_done rgate_done agate_psum")
        state_zeroed, st_mm, st_evac, kv_mm, state_step = sems("state_zeroed st_mm st_evac kv_mm state_step")
        ret_mm, ret_sq, ret_step, y_ret_psum, ret_mixed = sems("ret_mm ret_sq ret_step y_ret_psum ret_mixed")
        mixT_mm, mixhi_done, mixlo_done = sems("mixT_mm mixhi_done mixlo_done")
        h_part, h_added, h_gained, h_sq, h_step, left_ready, right_ready = sems(
            "h_part h_added h_gained h_sq h_step left_ready right_ready")

        def T(name):
            lo, hi = TAB[name]
            return tab[:, lo:hi]

        def x_part(m):
            return KQ if m == 0 else KH

        def x_parts(m, k):
            return (0 if m == 0 else KT // KQ + 2 * (m - 1)) + k // x_part(m) + 1

        def x_ps(m, k):
            b = {0: 2, 1: 6, 2: 2, 3: 4}[m] + k // x_part(m)
            return bank[b][:, (k % x_part(m)) * P:(k % x_part(m) + 1) * P]

        block = ctx.enter_context(nc.Block())

        def cols(b):
            return (b + 1) * P

        @block.sync
        def _(sp):
            def load_x(m):
                sp.dma_start(x_in[:, m, :], x[0, m * P:(m + 1) * P, :]).then_inc(x_loaded[m], 16)

            sp.dma_start(gain_rows, norm_gain[0].rearrange("(k p) -> k p", p=P)).then_inc(gain_in, 16)
            sp.dma_start(x_in[:, 0, 0:CW], x[0, 0:P, 0:CW]).then_inc(x0_left, 16)
            sp.dma_start(x_in[:, 0, CW:], x[0, 0:P, CW:]).then_inc(x_loaded[0], 16)
            for u in range(UNITS):
                src, w = unit_source(u, w_in, w_out)
                if u >= RAW:
                    sp.wait_ge(wlo_done, u - RAW + 1)
                dst = w_raw[:, u % RAW, :].rearrange("p (k c) -> p k c", k=KQ)[:, :, 0:w]
                sp.dma_start(dst, src).then_inc(raw_in[u % RAW], 16)
                if u == 1:
                    load_x(1)
                if u == QS - 1:
                    load_x(2)
                    load_x(3)
                    sp.dma_start(tab[:, :], table).then_inc(tab_in, 16)
            sp.wait_ge(ret_mm, MT)
            sp.dma_start(x_again[:, 0, :], x[0, 0:P, 0:CW]).then_inc(again_in[0], 16)
            sp.dma_start(fgain, final_gain.rearrange("(a d) -> a d", a=1).broadcast_to([P, D_MODEL])).then_inc(fgain_in, 16)
            for i in range(1, OUT_CH * MT):
                n, m = i // MT, i % MT
                if i >= 4:
                    sp.wait_ge(h_gained, i - 3)
                    sp.wait_ge(h_sq, i - 3)
                sp.dma_start(x_again[:, i % 4, :], x[0, m * P:(m + 1) * P, n * CW:(n + 1) * CW]).then_inc(again_in[i % 4], 16)
            for m in range(MT):
                sp.wait_ge(left_ready, m + 1)
                sp.dma_start(out[0, m * P:(m + 1) * P, 0:LEFT], h_out[:, m, 0:LEFT]).then_inc(left_stored, 16)
            sp.wait_ge(left_stored, 16 * MT)
            sp.wait_ge(right_stored, 16 * MT)

        @block.tensor
        def _(pe):
            pe.wait_ge(warm_up_zero, 1)
            for i in range(WARM_UP):
                pe.matmul(proj_ps[0][:, 0:P], th[:, 0:P], th[:, 0:P], start=True, stop=True)
            pe.wait_ge(ident_done, 1)
            pe.wait_ge(gain_in, 16)
            pe.transpose(mid_ps[:, 0:KT], gain_rows, ident[0:KT, 0:KT]).then_inc(gain_t, 1)

            def transpose_x(m):
                pe.wait_ge(x_loaded[m] if m else x0_left, 16)
                for k in range(KT):
                    if m == 0 and k == KH:
                        pe.wait_ge(x_loaded[0], 16)
                    if k == 0 and m == 1:
                        pe.wait_ge(gain_ok, 1)
                    if k == 0 and m >= 2:
                        pe.wait_ge(xlo_done, KT)
                    mm = pe.transpose(x_ps(m, k), x_in[:, m, k * P:(k + 1) * P], ident)
                    if k % x_part(m) == x_part(m) - 1:
                        mm.then_inc(xt_done, 1)

            transpose_x(0)

            def proj(g, q):
                if g < GROUPS:
                    c, m, c0, w = g // MT, g % MT, 0, CHUNKS[g // MT][2]
                else:
                    m, c0, w = OUT_PIECES[g - GROUPS]
                    c, c0 = NCH + c0 // CW, c0 % CW
                u = QS * c + q
                if q == 0:
                    if 2 <= g < MT * C_RG + 2:
                        pe.wait_ge(z_done, g - 1)
                    elif MT * C_RG + 2 <= g < MT * C_AG + 2:
                        pe.wait_ge(rgate_done, g - 2 - MT * C_RG + 1)
                    elif MT * C_AG + 2 <= g < GROUPS + 2:
                        pe.wait_ge(agate_psum, g - 2 - MT * C_AG + 1)
                    elif g >= GROUPS + 2:
                        pe.wait_ge(h_added, g - 2 - GROUPS + 1)
                    if g >= GROUPS:
                        pe.wait_ge(mixlo_done, 2 * (m + 1))
                if g < MT:
                    pe.wait_ge(xlo_done, KT * g + KQ * (q + 1))
                pe.wait_ge(wlo_done, u + 1)
                o = proj_ps[g % 2][:, 0:w]
                hi = w_hi[:, u % RING, :].rearrange("p (k c) -> p k c", k=KQ)
                lo = w_lo[:, u % RING, :].rearrange("p (k c) -> p k c", k=KQ)
                for kk in range(KQ):
                    k = KQ * q + kk
                    xh, xl = (t[:, k, m * P:(m + 1) * P] for t in (xT_hi, xT_lo))
                    first, last = k == 0, k == KT - 1
                    pe.matmul(o, xh, hi[:, kk, c0:c0 + w], start=first, stop=False)
                    pe.matmul(o, xh, lo[:, kk, c0:c0 + w], start=False, stop=False)
                    mm = pe.matmul(o, xl, hi[:, kk, c0:c0 + w], start=False, stop=last)
                if q == QS - 1:
                    mm.then_inc(proj_done, 1)
                elif m == MT - 1:
                    mm.then_inc(w_used, 1)

            def transpose_group(g):
                i = transposed(g)
                if i is None:
                    return
                pe.wait_ge(rope_done, i + 1)
                if i == 0:
                    pe.wait_ge(xlo_done, 2 * KT)
                if i >= 1:
                    pe.wait_ge(t_evac, i)
                    pe.wait_ge(idx_lo_done, min(i, MT))
                if 2 * MT < i <= 3 * MT:
                    pe.wait_ge(klo_done, i - 2 * MT)
                for j in range(3 if g < MT else 4):
                    mm = pe.transpose(mid_ps[:, j * P:(j + 1) * P], zt[:, g % 2, j * P:(j + 1) * P], ident)
                mm.then_inc(t_done, 1)

            def index_logits(b):
                pe.wait_ge(idx_lo_done, b + 1)
                for h in range(IDX_HEADS):
                    n = IDX_HEADS * (b - 1) + h
                    if n >= IDX_HEADS:
                        pe.wait_ge(relu_done, n - IDX_HEADS + 1)
                    else:
                        pe.wait_ge(xlo_done, MT * KT)
                    q, o = idx_q[:, h, b * P:(b + 1) * P], idx_ps[h][:, 0:cols(b)]
                    pe.matmul(o, q, idx_kh[:, 0:cols(b)], start=True, stop=False)
                    pe.matmul(o, q, idx_kl[:, 0:cols(b)], start=False, stop=True).then_inc(idx_mm, 1)

            def values(s):
                b, p = s // PAIRS, s % PAIRS
                if p == 0 and b >= 1:
                    pe.wait_ge(y_att_psum, b)
                for hh in range(2):
                    h = 2 * p + hh
                    pe.wait_ge(pt_evac, 2 * s + hh + 1)
                    for j in range(b + 1):
                        mm = pe.matmul(att_ps[:, h * HD:(h + 1) * HD], probT[:, hh, j * P:(j + 1) * P],
                                       v_att[:, j, h * HD:(h + 1) * HD], start=(j == 0), stop=(j == b))
                mm.then_inc(pv_done, 1)

            def transpose_probs(s):
                b = s // PAIRS
                for hh in range(2):
                    pe.wait_ge(exp_done, 2 * s + hh + 1)
                    if s >= 1:
                        pe.wait_ge(pt_evac, 2 * s + hh - 1)
                    for m in range(MT):
                        if s == steps_before_mix(m):
                            pe.wait_ge(mixlo_done, 2 * m + hh + 1)
                    for j in range(b + 1):
                        mm = pe.transpose(trans_ps[hh][:, j * P:(j + 1) * P], prob[:, hh, j * P:(j + 1) * P], ident)
                    mm.then_inc(pt_done, 1)

            def scores(s):
                b, p = s // PAIRS, s % PAIRS
                pe.wait_ge(klo_done, MT)
                pe.wait_ge(q_lo_done, b + 1)
                for hh in range(2):
                    if s == 0:
                        pe.wait_ge(relu_done, IDX_HEADS * (MT - 1))
                    else:
                        pe.wait_ge(max_done, 2 * s + hh - 1)
                    h, o = 2 * p + hh, score_ps[hh][:, 0:cols(b)]
                    pe.matmul(o, q_hl[:, h, :], k_stack[:, h, 0:cols(b)], start=True, stop=False)
                    pe.matmul(o, q_lh[:, h, :], k_stack[:, h, 0:cols(b)], start=False, stop=True).then_inc(qk_done, 1)

            def ret_scores(n, hh):
                r = slice(64 * hh, 64 * hh + 64)
                if hh:
                    pe.wait_ge(st_mm, 2 * n + 1)
                else:
                    pe.wait_ge(t_evac, 4 * MT)
                    if n >= 1:
                        pe.wait_ge(y_ret_psum, n)
                for h in (hh, hh + 2):
                    mm = pe.matmul(mid_ps[:, h * P:(h + 1) * P], krT[r, h // 2, n * P:(n + 1) * P],
                                   qrT[r, h // 2, n * P:(n + 1) * P], start=True, stop=True)
                mm.then_inc(st_mm, 1)

            def ret_kv(n):
                pe.wait_ge(st_evac, n + 1)
                for h in range(RH):
                    r = 64 * (h % 2)
                    mm = pe.matmul(mid_ps[r:r + 64, (h // 2) * RV:(h // 2 + 1) * RV],
                                   kz[:, n, h * RQK:(h + 1) * RQK], v_ret[:, n, h * RV:(h + 1) * RV],
                                   start=True, stop=True)
                mm.then_inc(kv_mm, 1)

            def ret_out(n):
                pe.wait_ge(st_evac, n + 1)
                pe.wait_ge(state_step, RH * min(n + 1, MT - 1))
                for p in range(2):
                    if n:
                        pe.matmul(mid_ps[:, 2 * p * RV:2 * (p + 1) * RV], qxT[:, p, n * P:(n + 1) * P],
                                  state[:, (n - 1) % 2, p, :], start=True, stop=False)
                    for h in (2 * p, 2 * p + 1):
                        mm = pe.matmul(mid_ps[:, h * RV:(h + 1) * RV], st_sb[:, h * P:(h + 1) * P],
                                       v_ret[:, n, h * RV:(h + 1) * RV], start=(n == 0), stop=(n == 0 or h % 2 == 1))
                mm.then_inc(ret_mm, 1)

            def transpose_mix(m):
                pe.wait_ge(att_mixed, m + 1)
                pe.wait_ge(ret_mixed, m + 1)
                pe.wait_ge(pt_evac, 2 * steps_before_mix(m))
                for half in range(2):
                    if m >= 1:
                        pe.wait_ge(mixlo_done, 2 * (m - 1) + half + 1)
                    for j in range(KH):
                        e = (KH * half + j) * P
                        mm = pe.transpose(trans_ps[half][:, j * P:(j + 1) * P], mix[:, m, e:e + P], ident)
                    mm.then_inc(mixT_mm, 1)

            for g in range(GROUPS + OUT_GROUPS):
                proj(g, 0)
                proj(g, 1)
                if g == 0:
                    transpose_x(1)
                if g >= RET0 + 1 and (g - RET0) % 2 == 1 and (g - RET0) // 2 < MT - 1:
                    ret_kv((g - RET0) // 2)
                if 0 <= g - (GROUPS - 1) < MT:
                    transpose_mix(g - (GROUPS - 1))
                transpose_group(g - 2)
                proj(g, 2)
                proj(g, 3)
                if g == 0:
                    transpose_x(2)
                    transpose_x(3)
                if MT <= g < 2 * MT - 1:
                    index_logits(g - MT + 1)
                retention = RET0 <= g < RET0 + 2 * MT
                if 0 <= g - ATT0 - 2 < STEPS:
                    values(g - ATT0 - 2)
                if retention and (g - RET0) % 2 == 0:
                    ret_scores((g - RET0) // 2, 0)
                if 0 <= g - ATT0 - 1 < STEPS:
                    transpose_probs(g - ATT0 - 1)
                if retention and (g - RET0) % 2 == 0:
                    ret_scores((g - RET0) // 2, 1)
                if 0 <= g - ATT0 < STEPS:
                    scores(g - ATT0)
                if retention and (g - RET0) % 2:
                    n = (g - RET0) // 2
                    if n == 1:
                        pe.wait_ge(qx_done, MT)
                    ret_out(n)

        @block.scalar
        def _(act):
            def split_hi(u):
                w = unit_source(u, w_in, w_out)[1]
                act.wait_ge(raw_in[u % RAW], 16 * (u // RAW + 1))
                if u >= RING:
                    c, q = (u - RING) // QS, (u - RING) % QS
                    if q == QS - 1:
                        act.wait_ge(proj_done, MT * (c + 1))
                    else:
                        act.wait_ge(w_used, (QS - 1) * c + q + 1)
                s, d = (t.rearrange("p (k c) -> p k c", k=KQ)[:, :, 0:w] for t in (w_raw[:, u % RAW, :], w_hi[:, u % RING, :]))
                act.activation(d, s, ACT.Copy).then_inc(whi_done, 1)

            def square_x(m):
                act.wait_ge(x_loaded[m], 16)
                if m == 0:
                    act.wait_ge(x0_left, 16)
                act.activation(mix[:, m, :], x_in[:, m, :], ACT.Square, scale=D_MODEL ** -0.5,
                               accum_out=ssq[:, m:m + 1]).then_inc(sq_even, 1)

            def x_hi(m, ks=range(KT)):
                for k in ks:
                    act.wait_ge(xt_done, x_parts(m, k))
                    act.activation(xT_hi[:, k, m * P:(m + 1) * P], x_ps(m, k), ACT.Copy,
                                   scale=gain[:, k:k + 1]).then_inc(xhi_done, 1)

            act.wait_ge(ident_done, 1)
            act.activation(junk[:, 0:1], ident[:, 0:1], ACT.Exp).then_inc(warmed, 1)
            act.wait_ge(gain_ok, 1)
            for u in range(QS):
                x_hi(0, range(KQ * u, KQ * (u + 1)))
                split_hi(u)
            x_hi(1)
            square_x(0)
            square_x(2)
            x_hi(2)

            def project_out(g):
                c, m = g // MT, g % MT
                act.wait_ge(proj_done, g + 1)
                act.wait_ge(hrstd_done, m + 1)
                src = proj_ps[g % 2]
                scale = rstd[:, m:m + 1]
                i = transposed(g)
                if i is not None:
                    if i >= 2:
                        act.wait_ge(t_done, i - 1)
                    w = 5 * IDX_DIM if c == 0 else CW
                    if c == 0:
                        act.activation(w_idx[:, m, :], src[:, w:w + IDX_HEADS], ACT.Copy, scale=scale).then_inc(w_idx_done, 1)
                    act.activation(zt[:, g % 2, 0:w], src[:, 0:w], ACT.Copy, scale=scale).then_inc(z_done, 1)
                elif c in (C_V, C_RV):
                    dst = (v_att if c == C_V else v_ret)[:, m, :]
                    act.activation(dst, src[:, :], ACT.Copy, scale=scale).then_inc(z_done, 1)
                else:
                    i = g - MT * C_RG
                    if i > MT:
                        act.wait_ge(agate_psum, i - MT)
                    elif i:
                        act.wait_ge(rgate_done, i)
                    else:
                        act.wait_ge(rope_done, 4 * MT)
                    act.activation(th[:, :], src[:, :], ACT.Tanh, scale=half_rstd[:, m:m + 1]).then_inc(tanh_done, 1)

            def transposed_out(g):
                i = transposed(g)
                if i is None:
                    return
                c, m = g // MT, g % MT
                t = slice(m * P, (m + 1) * P)
                act.wait_ge(t_done, i + 1)
                if c == 0:
                    for hh in range(2):
                        act.activation(idx_q[0:64, hh::2, t], mid_ps[64 * hh:64 * hh + 64, 0:2 * P].rearrange(
                            "p (a t) -> p a t", a=2), ACT.Copy)
                    act.activation(idx_kh[:, t], mid_ps[:, 2 * P:3 * P], ACT.Copy).then_inc(t_evac, 1)
                    return
                if c == 2:
                    if i == 2 * MT:
                        act.wait_ge(xt_done, x_parts(MT - 1, KT - 1))
                        act.wait_ge(sq_odd, 2)
                    for hh in range(2):
                        ins = act.activation(k_stack[0:64, hh::2, t], mid_ps[64 * hh:64 * hh + 64, :].rearrange(
                            "p (a t) -> p a t", a=PAIRS), ACT.Copy)
                    ins.then_inc(t_evac, 1)
                    return
                if i == 3 * MT:
                    act.wait_ge(idx_mm, IDX_HEADS * (MT - 1))
                src = mid_ps[:, :].rearrange("p (a t) -> p a t", a=4)
                dst = {1: qT, C_RQK: retT[:, 0:4, :]}[c][:, :, t]
                act.activation(dst, src, ACT.Copy).then_inc(t_evac, 1)

            def relus(b):
                for h in range(IDX_HEADS):
                    n = IDX_HEADS * (b - 1) + h
                    act.wait_ge(idx_mm, n + 1)
                    if b >= 2:
                        act.wait_ge(score_step, 5 * (b - 2) + h + 1)
                    act.activation(work[:, h, 0:cols(b)], idx_ps[h][:, 0:cols(b)], ACT.Relu).then_inc(relu_done, 1)

            def block_q_hi(b):
                if b:
                    act.wait_ge(qk_done, HEADS * b)
                for dst, r in ((q_hl, 0), (q_lh, 64)):
                    for hh in range(2):
                        ins = act.activation(dst[r:r + 64, hh::2, :], qT[64 * hh:64 * hh + 64, :, b * P:(b + 1) * P], ACT.Copy)
                ins.then_inc(q_hi_done, 1)

            def exps(s):
                b, p = s // PAIRS, s % PAIRS
                act.wait_ge(negmax_done, s + 1)
                if p == 0 and b >= 2:
                    act.wait_ge(y_att_psum, b - 1)
                for hh in range(2):
                    pr = prob[:, hh, 0:cols(b)]
                    act.activation(pr, pr, ACT.Exp, bias=neg_max[:, hh:hh + 1], scale=HD ** -0.5,
                                   accum_out=den[:, b % 2, 2 * p + hh:2 * p + hh + 1]).then_inc(exp_done, 1)

            def probT_out(s):
                b = s // PAIRS
                for hh in range(2):
                    act.wait_ge(pt_done, 2 * s + hh + 1)
                    if s >= 1:
                        act.wait_ge(pv_done, s)
                    elif hh == 0:
                        act.wait_ge(score_step, 5 * (MT - 1))
                    act.activation(probT[:, hh, 0:cols(b)], trans_ps[hh][:, 0:cols(b)], ACT.Copy).then_inc(pt_evac, 1)

            def ret_squares(n):
                act.wait_ge(ret_mm, n + 1)
                if n == 0:
                    act.wait_ge(warmed, 1)
                for h in range(RH):
                    if h == 0 and n:
                        act.wait_ge(ret_step, 3 * n)
                        act.wait_ge(ret_sq, RH * n)
                    act.activation(junk[:, h * RV:(h + 1) * RV], mid_ps[:, h * RV:(h + 1) * RV], ACT.Square, scale=RV ** -0.5,
                                   accum_out=ret_ms[:, h:h + 1]).then_inc(ret_sq, 1)

            def mix_hi(m):
                act.wait_ge(proj_done, GROUPS - MT + m + 1)
                for half in range(2):
                    act.wait_ge(mixT_mm, 2 * m + half + 1)
                    act.activation(xT_hi[:, KH * half:KH * (half + 1), m * P:(m + 1) * P],
                                   trans_ps[half][:, :].rearrange("p (k t) -> p k t", k=KH), ACT.Copy).then_inc(mixhi_done, 1)

            for g in range(GROUPS + OUT_GROUPS):
                for u in splits_at(g, "start"):
                    split_hi(u)
                if 0 <= g - (GROUPS - 1) < MT:
                    mix_hi(g - (GROUPS - 1))
                transposed_out(g - 2)
                for u in splits_at(g, "middle"):
                    split_hi(u)
                if g < GROUPS:
                    project_out(g)
                if g == 0:
                    x_hi(3)
                if MT <= g < 2 * MT - 1:
                    relus(g - MT + 1)
                if 0 <= g - ATT0 - 1 < STEPS:
                    probT_out(g - ATT0 - 1)
                if 0 <= g - ATT0 < STEPS:
                    exps(g - ATT0)
                if RET0 <= g < RET0 + 2 * MT and (g - RET0) % 2 == 1:
                    ret_squares((g - RET0) // 2)
                if block_split_at(g) is not None:
                    block_q_hi(block_split_at(g))
                if g >= GROUPS:
                    i = g - GROUPS
                    act.wait_ge(h_added, i + 1)
                    if i:
                        act.wait_ge(h_sq, i)
                    else:
                        act.wait_ge(ret_sq, RH * MT)
                    m, c0, w = OUT_PIECES[i]
                    complete = c0 + w == D_MODEL
                    tile, c0 = c0 // CW * MT + m, c0 % CW
                    act.activation(junk[:, 0:w], x_again[:, tile % 4, c0:c0 + w], ACT.Square,
                                   scale=D_MODEL ** -0.5, accum_out=out_ms[:, i:i + 1]).then_inc(h_sq, 1)
                    if complete:
                        right = h_out[:, m, LEFT:D_MODEL]
                        act.wait_ge(h_gained, i + 1)
                        act.wait_ge(h_step, 2 * m + 2)
                        act.activation(right, right, ACT.Copy, scale=out_rstd[:, m:m + 1]).then_inc(right_ready, 1)
                        act.wait_ge(right_ready, m + 1)
                        act.dma_start(out[0, m * P:(m + 1) * P, LEFT:D_MODEL], right).then_inc(right_stored, 16)

        @block.gpsimd
        def _(pool):
            step = 0

            def xi_times_q(m):
                t = slice(m * P, (m + 1) * P)
                pool.wait_ge(t_evac, 3 * MT + m + 1)
                pool.tensor_tensor(qxT[:, :, t], qrT[:, :, t], T("xi").rearrange("p (a t) -> p a t", a=2),
                                   ALU.mult).then_inc(qx_done, 1)

            def chain(ins):
                nonlocal step
                step += 1
                ins.then_inc(rope_step, 1)
                return step

            def rsqrt(out, ms, eps_at, done, count, more=None):
                n = ms.shape[1]
                if more is None:
                    pool.tensor_scalar(eps_at, ms, EPS, None, ALU.add).then_inc(done, 1)
                else:
                    pool.tensor_scalar(eps_at, ms, more, EPS, ALU.add, ALU.add).then_inc(done, 1)
                pool.wait_ge(done, count + 1)
                pool.tensor_tensor(out, eps_at, minus_half[:, 0:n], ALU.pow).then_inc(done, 1)
                pool.wait_ge(done, count + 2)

            pool.memset(ident, 0.0).then_inc(ident_zero, 1)
            pool.wait_ge(ident_zero, 1)
            pool.affine_select(out=ident, in_=ident, compare_op=ALU.not_equal, fill=1.0, base=0,
                               pattern=[[-1, P]], channel_multiplier=1).then_inc(ident_done, 1)
            pool.memset(minus_half, -0.5).then_inc(minus_half_done, 1)
            pool.wait_ge(minus_half_done, 1)

            def x_rstd(m):
                pool.wait_ge(sq_odd if m % 2 else sq_even, m // 2 + 1)
                c = slice(m, m + 1)
                rsqrt(rstd[:, c], ssq[:, c], ms_eps[:, c], rstd_done, 2 * m)
                pool.tensor_scalar(half_rstd[:, c], rstd[:, c], 0.5, None, ALU.mult).then_inc(hrstd_done, 1)

            for g in range(GROUPS):
                i = transposed(g)
                if i is None:
                    continue
                c, m = g // MT, g % MT
                if c == 0:
                    x_rstd(m)
                ret = c == C_RQK
                heads = 5 if c == 0 else 8
                half = RET_HALF if ret else ROPE_HALF
                z4 = zt[:, g % 2, 0:heads * HD].rearrange("p (h d) -> p h d", h=heads)
                z = z4[:, :, 0:2 * half].rearrange("p h (s e) -> p h s e", s=2)
                ta = rope_a[:, 0:heads * 2 * half].rearrange("p (h s e) -> p h s e", h=heads, s=2)
                tb = rope_b[:, 0:heads * 2 * half].rearrange("p (h s e) -> p h s e", h=heads, s=2)
                cos = T("ret_cos" if ret else "att_cos")[:, m * half:(m + 1) * half]
                sin = T("ret_sin" if ret else "att_sin")[:, 2 * m * half:2 * (m + 1) * half]
                cos = cos.rearrange("p (h e) -> p h e", h=1).broadcast_to([P, heads, half])
                sin = sin.rearrange("p (h s e) -> p h s e", h=1, s=2)
                pool.wait_ge(tab_in, 16)
                zg = g + 1
                pool.wait_ge(z_done, zg)
                pool.wait_ge(rope_done, i) if i else None
                for s in range(2):
                    chain(pool.tensor_tensor(ta[:, :, s, :], z[:, :, s, :], cos, ALU.mult))
                    last = chain(pool.tensor_tensor(tb[:, :, s, :], z[:, :, 1 - s, :],
                                                    sin[:, :, s, :].broadcast_to([P, heads, half]), ALU.mult))
                pool.wait_ge(rope_step, last)
                add = pool.tensor_tensor(z, ta, tb, ALU.add)
                if c in (1, 2):
                    add.then_inc(rope_done, 1)
                    continue
                last = chain(add)
                pool.wait_ge(rope_step, last)
                if c == 0:
                    pool.tensor_copy(zt[:, g % 2, 5 * HD:6 * HD], zt[:, g % 2, 4 * HD:5 * HD]).then_inc(rope_done, 1)
                else:
                    pool.tensor_tensor(kz[:, m, :].rearrange("p (h d) -> p h d", h=RH), z4[:, RH:2 * RH, :],
                                       T("zeta").rearrange("p (h d) -> p h d", d=1).broadcast_to([P, RH, RQK]),
                                       ALU.mult).then_inc(rope_done, 1)
                    if m:
                        xi_times_q(m - 1)
            xi_times_q(MT - 1)
            pool.wait_ge(t_done, 4 * MT)
            pool.memset(zt[:, :, :], 0.0).then_inc(state_zeroed, 1)

            for n in range(MT):
                pool.wait_ge(ret_sq, RH * (n + 1))
                rsqrt(ret_r, ret_ms, ms_eps, ret_step, 3 * n)
                if n:
                    pool.wait_ge(y_ret_psum, n)
                pool.tensor_scalar(rcoef, ret_r, half_rstd[:, n:n + 1], None, ALU.mult).then_inc(ret_step, 1)
                pool.wait_ge(ret_step, 3 * n + 3)
            for m in range(MT):
                pool.wait_ge(h_sq, MT + m + 1)
                left, right = out_ms[:, m:m + 1], out_ms[:, MT + m:MT + m + 1]
                if m == MT - 1:
                    pool.tensor_tensor(right, right, left, ALU.add).then_inc(h_part, 1)
                    pool.wait_ge(h_part, 1)
                    left = out_ms[:, OUT_GROUPS - 1:OUT_GROUPS]
                    pool.wait_ge(h_sq, OUT_GROUPS)
                rsqrt(out_rstd[:, m:m + 1], left, out_ms1[:, m:m + 1], h_step, 2 * m, right)

        @block.vector
        def _(dve):
            def split_lo(u):
                w = unit_source(u, w_in, w_out)[1]
                dve.wait_ge(whi_done, u + 1)
                s, h, d = (t.rearrange("p (k c) -> p k c", k=KQ)[:, :, 0:w]
                           for t in (w_raw[:, u % RAW, :], w_hi[:, u % RING, :].bitcast(F32), w_lo[:, u % RING, :]))
                dve.tensor_tensor(d, s, h, ALU.subtract).then_inc(wlo_done, 1)

            dve.memset(th[:, 0:P], 0.0).then_inc(warm_up_zero, 1)
            dve.wait_ge(gain_t, 1)
            dve.tensor_copy(gain, mid_ps[:, 0:KT]).then_inc(gain_ok, 1)
            dve.wait_ge(gain_ok, 1)
            def x_lo(m, ks=range(KT)):
                for k in ks:
                    dve.wait_ge(xhi_done, KT * m + x_part(m) * (k // x_part(m) + 1))
                    t = slice(m * P, (m + 1) * P)
                    dve.scalar_tensor_tensor(out=xT_lo[:, k, t], in0=x_ps(m, k), scalar=gain[:, k:k + 1],
                                             in1=xT_hi[:, k, t].bitcast(F32), op0=ALU.mult,
                                             op1=ALU.subtract).then_inc(xlo_done, 1)

            def square_x(m):
                dve.wait_ge(x_loaded[m], 16)
                dve.tensor_tensor_reduce(out=mix[:, m, :], in0=x_in[:, m, :], in1=x_in[:, m, :], scale=1.0 / D_MODEL,
                                         scalar=0.0, op0=ALU.mult, op1=ALU.add, accum_out=ssq[:, m:m + 1]).then_inc(sq_odd, 1)

            for u in range(QS):
                x_lo(0, range(KQ * u, KQ * (u + 1)))
                split_lo(u)
            x_lo(1)
            square_x(1)
            x_lo(2)
            square_x(3)
            x_lo(3)

            def index_lo(m):
                t = slice(m * P, (m + 1) * P)
                dve.wait_ge(t_evac, m + 1)
                for hh in range(2):
                    dve.tensor_tensor(idx_q[64:128, hh::2, t], mid_ps[64 * hh:64 * hh + 64, 0:2 * P].rearrange(
                        "p (a t) -> p a t", a=2), idx_q[0:64, hh::2, t].bitcast(F32), ALU.subtract)
                dve.tensor_tensor(idx_kl[:, t], mid_ps[:, 2 * P:3 * P], idx_kh[:, t].bitcast(F32),
                                  ALU.subtract).then_inc(idx_lo_done, 1)

            def key_lo(m):
                t = slice(m * P, (m + 1) * P)
                dve.wait_ge(t_evac, 2 * MT + m + 1)
                for hh in range(2):
                    ins = dve.tensor_tensor(k_stack[64:128, hh::2, t], mid_ps[64 * hh:64 * hh + 64, :].rearrange(
                        "p (a t) -> p a t", a=PAIRS), k_stack[0:64, hh::2, t].bitcast(F32), ALU.subtract)
                ins.then_inc(klo_done, 1)

            def block_q_lo(b):
                dve.wait_ge(q_hi_done, b + 1)
                for dst, r in ((q_hl, 64), (q_lh, 0)):
                    for hh in range(2):
                        upper = (q_hl[0:64, 0::2, :], q_lh[64:128, 1::2, :])[hh]
                        ins = dve.tensor_tensor(dst[r:r + 64, hh::2, :], qT[64 * hh:64 * hh + 64, :, b * P:(b + 1) * P],
                                                upper.bitcast(F32), ALU.subtract)
                ins.then_inc(q_lo_done, 1)

            def index_scores(b):
                dve.wait_ge(w_idx_done, b + 1)
                for h in range(IDX_HEADS):
                    dve.wait_ge(relu_done, IDX_HEADS * (b - 1) + h + 1)
                    src, w = work[:, h, 0:cols(b)], w_idx[:, b, h:h + 1]
                    if h == 0:
                        ins = dve.tensor_scalar(keys[b][:, :], src, w, None, ALU.mult)
                    else:
                        dve.wait_ge(score_step, 5 * (b - 1) + h)
                        ins = dve.scalar_tensor_tensor(out=keys[b][:, :], in0=src, scalar=w, in1=keys[b][:, :],
                                                       op0=ALU.mult, op1=ALU.add)
                    ins.then_inc(score_step, 1)
                dve.wait_ge(score_step, 5 * (b - 1) + 4)
                diag = keys[b][:, b * P:(b + 1) * P]
                dve.tensor_tensor(diag, diag, T("causal"), ALU.add).then_inc(score_step, 1)

            def topk_round(r):
                b = 1 + r // ROUNDS
                dve.wait_ge(round_step, 2 * r) if r else None
                dve.wait_ge(score_step, 5 * b)
                dve.max(top8[:, :], keys[b][:, :]).then_inc(round_step, 1)
                dve.wait_ge(round_step, 2 * r + 1)
                dve.match_replace(keys[b][:, :], top8[:, :], keys[b][:, :], TAKEN).then_inc(round_step, 1)
                if r % ROUNDS == ROUNDS - 1:
                    dve.wait_ge(round_step, 2 * r + 2)
                    dve.tensor_scalar(keys[b][:, :], keys[b][:, :], NEVER, MASKED, ALU.is_gt, ALU.mult).then_inc(mask_done, 1)

            def masked_max(s):
                b = s // PAIRS
                dve.wait_ge(mask_done, b) if b else None
                if s:
                    dve.wait_ge(negmax_done, s)
                    dve.wait_ge(exp_done, 2 * s)
                for hh in range(2):
                    dve.wait_ge(qk_done, 2 * s + hh + 1)
                    if s:
                        dve.wait_ge(pt_done, 2 * s + hh - 1)
                    if b == 0:
                        mask, o = T("causal"), prob[:, hh, 0:P]
                    else:
                        mask, o = keys[b][:, :], prob[:, hh, 0:cols(b)]
                    dve.tensor_tensor_reduce(out=o, in0=score_ps[hh][:, 0:cols(b)], in1=mask, scale=1.0, scalar=TAKEN,
                                             op0=ALU.add, op1=ALU.max, accum_out=row_max[:, hh:hh + 1]).then_inc(max_done, 1)
                dve.wait_ge(max_done, 2 * s + 2)
                dve.tensor_scalar(neg_max, row_max, -(HD ** -0.5), None, ALU.mult).then_inc(negmax_done, 1)

            tmp_last_read = [None]

            def gate(g):
                i = g - MT * C_RG
                m, ret = i % MT, i < MT
                dve.wait_ge(tanh_done, i + 1)
                w = slice(ATT_W, 2 * ATT_W) if ret else slice(0, ATT_W)
                straight = ret or m == MT - 1
                if not straight and tmp_last_read[0]:
                    dve.wait_ge(*tmp_last_read[0])
                dst = mix[:, m, w] if straight else tmp[:, :]
                dve.scalar_tensor_tensor(out=dst, in0=th[:, :], scalar=1.0, in1=proj_ps[g % 2][:, :], op0=ALU.add,
                                         op1=ALU.mult).then_inc(rgate_done if ret else agate_psum, 1)
                if not straight:
                    dve.wait_ge(agate_psum, m + 1)
                    dve.wait_ge(y_att_psum, m + 1)
                    dve.tensor_tensor(mix[:, m, w], mix[:, m, w], tmp[:, :], ALU.mult).then_inc(att_mixed, 1)
                    tmp_last_read[0] = (att_mixed, m + 1)

            def attention_out(b):
                dve.wait_ge(pv_done, PAIRS * (b + 1))
                dve.wait_ge(exp_done, 2 * PAIRS * (b + 1))
                if b:
                    dve.wait_ge(y_att_psum, b)
                dve.reciprocal(rden, den[:, b % 2, :]).then_inc(att_step, 1)
                dve.wait_ge(att_step, 2 * b + 1)
                dve.tensor_scalar(acoef, rden, half_rstd[:, b:b + 1], None, ALU.mult).then_inc(att_step, 1)
                dve.wait_ge(att_step, 2 * b + 2)
                co = acoef.rearrange("p (h d) -> p h d", d=1).broadcast_to([P, HEADS, HD])
                src = att_ps[:, :].rearrange("p (h d) -> p h d", h=HEADS)
                half = mix[:, b, 0:ATT_W]
                if b < MT - 1:
                    dve.tensor_tensor(half.rearrange("p (h d) -> p h d", h=HEADS), src, co, ALU.mult).then_inc(y_att_psum, 1)
                else:
                    dve.wait_ge(*tmp_last_read[0])
                    dve.tensor_tensor(tmp[:, :].rearrange("p (h d) -> p h d", h=HEADS), src, co, ALU.mult).then_inc(y_att_psum, 1)
                    dve.wait_ge(y_att_psum, b + 1)
                    dve.wait_ge(agate_psum, MT)
                    dve.tensor_tensor(half, half, tmp[:, :], ALU.mult).then_inc(att_mixed, 1)
                    tmp_last_read[0] = (att_mixed, MT)

            def decayed(n):
                dve.wait_ge(st_mm, 2 * n + 2)
                if n:
                    dve.wait_ge(ret_mm, n)
                dve.tensor_tensor(st_sb[:, :], mid_ps[:, :], T("decay"), ALU.mult).then_inc(st_evac, 1)

            def next_state(n):
                dve.wait_ge(kv_mm, n + 1)
                if n:
                    dve.wait_ge(state_step, RH * n)
                else:
                    dve.wait_ge(state_zeroed, 1)
                if n >= 2:
                    dve.wait_ge(ret_mm, n)
                for h in range(RH):
                    p, hh = h // 2, h % 2
                    r, w = slice(64 * hh, 64 * hh + 64), slice(hh * RV, (hh + 1) * RV)
                    kv = mid_ps[r, p * RV:(p + 1) * RV]
                    if n == 0:
                        ins = dve.tensor_copy(state[r, 0, p, w], kv)
                    else:
                        ins = dve.scalar_tensor_tensor(out=state[r, n % 2, p, w], in0=state[r, (n - 1) % 2, p, w],
                                                       scalar=T("g_chunk")[r, p:p + 1], in1=kv,
                                                       op0=ALU.mult, op1=ALU.add)
                    ins.then_inc(state_step, 1)

            def retention_out(n):
                dve.wait_ge(ret_step, 3 * n + 3)
                if tmp_last_read[0]:
                    dve.wait_ge(*tmp_last_read[0])
                dve.tensor_tensor(tmp[:, :].rearrange("p (h d) -> p h d", h=RH),
                                  mid_ps[:, :].rearrange("p (h d) -> p h d", h=RH),
                                  rcoef.rearrange("p (h d) -> p h d", d=1).broadcast_to([P, RH, RV]),
                                  ALU.mult).then_inc(y_ret_psum, 1)
                dve.wait_ge(y_ret_psum, n + 1)
                dve.wait_ge(rgate_done, n + 1)
                half = mix[:, n, ATT_W:2 * ATT_W]
                dve.tensor_tensor(half, half, tmp[:, :], ALU.mult).then_inc(ret_mixed, 1)
                tmp_last_read[0] = (ret_mixed, n + 1)

            def mix_lo(m):
                for half in range(2):
                    dve.wait_ge(mixhi_done, 2 * m + half + 1)
                    ks, t = slice(KH * half, KH * (half + 1)), slice(m * P, (m + 1) * P)
                    dve.tensor_tensor(xT_lo[:, ks, t], trans_ps[half][:, :].rearrange("p (k t) -> p k t", k=KH),
                                      xT_hi[:, ks, t].bitcast(F32), ALU.subtract).then_inc(mixlo_done, 1)

            def add_residual(i):
                m, c0, width = OUT_PIECES[i]
                w, tile, c0 = slice(c0, c0 + width), c0 // CW * MT + m, c0 % CW
                h = x_again[:, tile % 4, c0:c0 + width]
                dve.wait_ge(proj_done, GROUPS + i + 1)
                dve.wait_ge(again_in[tile % 4], 16 * (tile // 4 + 1))
                dve.tensor_tensor(h, proj_ps[i % 2][:, 0:width], h, ALU.add).then_inc(h_added, 1)
                dve.wait_ge(h_added, i + 1)
                dve.wait_ge(fgain_in, 16)
                if i == 0:
                    dve.wait_ge(qk_done, 2 * STEPS)
                dve.tensor_tensor(h_out[:, m, w], h, fgain[:, w], ALU.mult).then_inc(h_gained, 1)

            def normalise(m, i):
                dve.wait_ge(h_gained, i + 1)
                dve.wait_ge(h_step, 2 * m + 2)
                w = slice(0, LEFT)
                dve.tensor_scalar(h_out[:, m, w], h_out[:, m, w], out_rstd[:, m:m + 1], None, ALU.mult).then_inc(left_ready, 1)

            for g in range(GROUPS + OUT_GROUPS):
                for u in splits_at(g, "start"):
                    split_lo(u)
                if 0 <= g - 2 < MT:
                    index_lo(g - 2)
                if 0 <= g - 2 - 2 * MT < MT:
                    key_lo(g - 2 - 2 * MT)
                for u in splits_at(g, "middle"):
                    split_lo(u)
                if g >= RET0 + 1 and (g - RET0) % 2 == 1 and (g - RET0) // 2 < MT - 1:
                    next_state((g - RET0) // 2)
                if 0 <= g - (GROUPS - 1) < MT:
                    mix_lo(g - (GROUPS - 1))
                if MT * C_RG <= g < GROUPS:
                    gate(g)
                if g >= GROUPS:
                    add_residual(g - GROUPS)
                    m, c0, w = OUT_PIECES[g - GROUPS]
                    if c0 + w == D_MODEL:
                        normalise(m, g - GROUPS)
                if MT <= g < 2 * MT - 1:
                    index_scores(g - MT + 1)
                s = g - ATT0 - 2
                if 0 <= s < STEPS and s % PAIRS == PAIRS - 1:
                    attention_out(s // PAIRS)
                if RET0 <= g < RET0 + 2 * MT and (g - RET0) % 2 == 0:
                    decayed((g - RET0) // 2)
                if 0 <= g - ATT0 < STEPS:
                    masked_max(g - ATT0)
                if RET0 <= g < RET0 + 2 * MT and (g - RET0) % 2 == 1:
                    retention_out((g - RET0) // 2)
                if block_split_at(g) is not None:
                    block_q_lo(block_split_at(g))
                for r in rounds_at(g):
                    topk_round(r)

    return nc


_INS = ["x", "norm_gain", "w_in", "w_out", "final_gain"]


def kernel(**inputs):
    import concourse.bacc as bacc
    from concourse.bass_utils import run_bass_kernel_spmd

    nc = bacc.Bacc("TRN2", target_bir_lowering=False, num_devices=1)
    arrays = {n: np.ascontiguousarray(inputs[n]) for n in _INS}
    arrays["table"] = tables()
    args = [nc.dram_tensor(f"in_{n}", a.shape, mybir.dt.from_np(a.dtype), kind="ExternalInput").ap()
            for n, a in arrays.items()]
    out = nc.dram_tensor("out", (1, SEQ, D_MODEL), F32, kind="ExternalOutput").ap()
    hymba_layer(nc, *args, out)
    r = run_bass_kernel_spmd(nc, [{f"in_{n}": a for n, a in arrays.items()}], core_ids=[0])
    return r.results[0]["out"]
```
